# Optimizing a Trainium2 kernel written in Bass

```python
import jax, jax.numpy as jnp
from jax import lax
import numpy as np

D_MODEL = 1024
BATCH = 1
SEQ = 512
DEPTH = 2

PLE_DIM = 256
D_CONV = 512
N_CONV_GROUPS = 8
CONV_WIDTH = 31
N_RET_HEADS = 4
RET_HEAD_DIM = 128
D_RET = N_RET_HEADS * RET_HEAD_DIM
D_MIX = D_CONV + D_RET
D_IN_PROJ = 2 * D_CONV + 4 * D_RET
RET_CHUNK = 128
ROPE_BASE = 10000.0
D_FF = 2816
FFN_CONV_WIDTH = 3
EPS = 1e-6

kernel_name = "hybrid_conformer_retention_block"

def rms_norm(x, g):
    xf = x.astype(jnp.float32)
    y = xf * lax.rsqrt(jnp.mean(xf * xf, axis=-1, keepdims=True) + EPS)
    return (y * g.astype(jnp.float32)).astype(x.dtype)

def layer_norm(x, g, b):
    xf = x.astype(jnp.float32)
    mu = jnp.mean(xf, axis=-1, keepdims=True)
    var = jnp.mean(jnp.square(xf - mu), axis=-1, keepdims=True)
    y = (xf - mu) * lax.rsqrt(var + EPS)
    return (y * g.astype(jnp.float32) + b.astype(jnp.float32)).astype(x.dtype)

def causal_dwconv(x, w, b):
    k_width, ch = w.shape
    y = lax.conv_general_dilated(
        x, w[:, None, :].astype(x.dtype), window_strides=(1,),
        padding=[(k_width - 1, 0)], dimension_numbers=("NWC", "WIO", "NWC"),
        feature_group_count=ch)
    return y + b.astype(x.dtype)

def rotary_tables(positions):
    half = RET_HEAD_DIM // 2
    inv_freq = ROPE_BASE ** (-jnp.arange(half, dtype=jnp.float32) / half)
    ang = positions.astype(jnp.float32)[..., None] * inv_freq
    return jnp.cos(ang)[:, :, None, :], jnp.sin(ang)[:, :, None, :]

def apply_rotary(x, cos, sin):
    half = x.shape[-1] // 2
    x1, x2 = x[..., :half], x[..., half:]
    c, s = cos.astype(x.dtype), sin.astype(x.dtype)
    return jnp.concatenate([x1 * c - x2 * s, x2 * c + x1 * s], axis=-1)

def chunk_retention(q, k, v):
    bsz, seq, n_h, d_k = q.shape
    d_v = v.shape[-1]
    C = RET_CHUNK
    nc = seq // C
    log_g = jnp.log1p(-(2.0 ** (-5.0 - jnp.arange(n_h, dtype=jnp.float32))))
    idx = jnp.arange(C, dtype=jnp.float32)
    rel = idx[:, None] - idx[None, :]
    decay_in = jnp.where(rel >= 0, jnp.exp(log_g[:, None, None] * jnp.maximum(rel, 0.0)), 0.0).astype(q.dtype)
    zeta = jnp.exp(log_g[:, None] * (C - 1 - idx)).astype(q.dtype)
    xi = jnp.exp(log_g[:, None] * (idx + 1)).astype(q.dtype)
    chunk_decay = jnp.exp(log_g * C).astype(q.dtype)

    qc = q.reshape(bsz, nc, C, n_h, d_k)
    kc = k.reshape(bsz, nc, C, n_h, d_k)
    vc = v.reshape(bsz, nc, C, n_h, d_v)

    scores = jnp.einsum("bcnhd,bcmhd->bchnm", qc, kc) * decay_in
    inner = jnp.einsum("bchnm,bcmhe->bcnhe", scores, vc)

    kv = jnp.einsum("bcmhd,bcmhe,hm->cbhde", kc, vc, zeta)

    def step(state, kv_c):
        return state * chunk_decay[None, :, None, None] + kv_c, state

    _, state_prev = lax.scan(step, jnp.zeros_like(kv[0]), kv)
    cross = jnp.einsum("bcnhd,cbhde,hn->bcnhe", qc, state_prev, xi)
    return (inner + cross).reshape(bsz, seq, n_h, d_v)

def head_group_norm(o, g):
    of = o.astype(jnp.float32)
    mu = jnp.mean(of, axis=-1, keepdims=True)
    var = jnp.mean(jnp.square(of - mu), axis=-1, keepdims=True)
    y = ((of - mu) * lax.rsqrt(var + EPS)).reshape(o.shape[0], o.shape[1], -1)
    return (y * g.astype(jnp.float32)).astype(o.dtype)

def mixer(h, cos, sin, w_in, conv_w, conv_b, conv_ln_g, conv_ln_b, ret_gn_g, w_out):
    bsz, seq, _ = h.shape
    proj = h @ w_in
    splits = [D_CONV, 2 * D_CONV, 2 * D_CONV + D_RET, 2 * D_CONV + 2 * D_RET, 2 * D_CONV + 3 * D_RET]
    c_val, c_gate, q, k, v, g = jnp.split(proj, splits, axis=-1)

    u = c_val * jax.nn.sigmoid(c_gate)
    u = causal_dwconv(u, conv_w, conv_b)
    u = jax.nn.silu(layer_norm(u, conv_ln_g, conv_ln_b))

    q = apply_rotary(q.reshape(bsz, seq, N_RET_HEADS, RET_HEAD_DIM), cos, sin)
    k = apply_rotary(k.reshape(bsz, seq, N_RET_HEADS, RET_HEAD_DIM), cos, sin) * (RET_HEAD_DIM ** -0.5)
    v = v.reshape(bsz, seq, N_RET_HEADS, RET_HEAD_DIM)
    o = head_group_norm(chunk_retention(q, k, v), ret_gn_g)
    o = jax.nn.silu(g) * o

    return jnp.concatenate([u, o], axis=-1) @ w_out

def conv_gated_mlp(h, ffn_up, ffn_conv_w, ffn_conv_b, ffn_down):
    up = causal_dwconv(h @ ffn_up, ffn_conv_w, ffn_conv_b)
    val, gate = jnp.split(up, 2, axis=-1)
    return (jax.nn.gelu(gate, approximate=True) * val) @ ffn_down

def setup_inputs(seed: int = 0) -> dict:
    key = jax.random.key(seed)
    ks = jax.random.split(key, 24)
    f32 = jnp.float32
    L = DEPTH

    def nrm(k, shape, scale):
        return jax.random.normal(k, shape, f32) * scale

    def gain(k, shape):
        return 1.0 + 0.02 * jax.random.normal(k, shape, f32)

    x = jax.random.normal(ks[0], (BATCH, SEQ, D_MODEL), f32)
    p = jax.random.normal(ks[1], (DEPTH, BATCH, SEQ, PLE_DIM), f32)
    offset = jax.random.randint(ks[2], (BATCH, 1), 0, 4096, dtype=jnp.int32)
    positions = (offset + jnp.arange(SEQ, dtype=jnp.int32)[None, :]).astype(jnp.int32)
    return {
        "x": x,
        "p": p,
        "positions": positions,
        "norm_mix_pre": gain(ks[3], (L, D_MODEL)),
        "norm_mix_post": gain(ks[4], (L, D_MODEL)),
        "norm_ffn_pre": gain(ks[5], (L, D_MODEL)),
        "norm_ffn_post": gain(ks[6], (L, D_MODEL)),
        "w_in": nrm(ks[7], (L, D_MODEL, D_IN_PROJ), D_MODEL ** -0.5),
        "conv_w": nrm(ks[8], (L, CONV_WIDTH, D_CONV), CONV_WIDTH ** -0.5),
        "conv_b": nrm(ks[9], (L, D_CONV), 0.01),
        "conv_ln_g": gain(ks[10], (L, D_CONV)),
        "conv_ln_b": nrm(ks[11], (L, D_CONV), 0.01),
        "ret_gn_g": gain(ks[12], (L, D_RET)),
        "w_out": nrm(ks[13], (L, D_MIX, D_MODEL), D_MIX ** -0.5),
        "ffn_up": nrm(ks[14], (L, D_MODEL, 2 * D_FF), D_MODEL ** -0.5),
        "ffn_conv_w": nrm(ks[15], (L, FFN_CONV_WIDTH, 2 * D_FF), FFN_CONV_WIDTH ** -0.5),
        "ffn_conv_b": nrm(ks[16], (L, 2 * D_FF), 0.01),
        "ffn_down": nrm(ks[17], (L, D_FF, D_MODEL), D_FF ** -0.5),
        "ple_gate": nrm(ks[18], (L, D_MODEL, D_MODEL), D_MODEL ** -0.5),
        "ple_proj": nrm(ks[19], (L, PLE_DIM, D_MODEL), PLE_DIM ** -0.5),
    }

def reference(x, p, positions, norm_mix_pre, norm_mix_post, norm_ffn_pre, norm_ffn_post,
              w_in, conv_w, conv_b, conv_ln_g, conv_ln_b, ret_gn_g, w_out,
              ffn_up, ffn_conv_w, ffn_conv_b, ffn_down, ple_gate, ple_proj):
    cos, sin = rotary_tables(positions)
    for i in range(DEPTH):
        h = rms_norm(x, norm_mix_pre[i])
        m = mixer(h, cos, sin, w_in[i], conv_w[i], conv_b[i], conv_ln_g[i], conv_ln_b[i],
                  ret_gn_g[i], w_out[i])
        x = x + rms_norm(m, norm_mix_post[i])
        h = rms_norm(x, norm_ffn_pre[i])
        f = conv_gated_mlp(h, ffn_up[i], ffn_conv_w[i], ffn_conv_b[i], ffn_down[i])
        x = x + rms_norm(f, norm_ffn_post[i])
        x = x + jax.nn.sigmoid(x @ ple_gate[i]) * (p[i] @ ple_proj[i])
    return x


_drawn_inputs = setup_inputs


def setup_inputs(seed=0):
    import zlib

    import numpy as np

    out = dict(_drawn_inputs(seed))
    spreads = {}
    factors = {'norm_ffn_post': 3.365,
     'conv_b': 3.324,
     'conv_ln_g': 3.032,
     'conv_ln_b': 6.726,
     'ret_gn_g': 3.635,
     'ffn_conv_b': 4.84}
    for name, (base, spread) in spreads.items():
        noise = np.random.default_rng([zlib.crc32(name.encode()), seed]).standard_normal(out[name].shape)
        drawn = base * np.exp(spread * noise) if base else spread * noise
        out[name] = __import__('jax').numpy.asarray(drawn.astype(out[name].dtype))
    for name, factor in factors.items():
        out[name] = (out[name] * factor).astype(out[name].dtype)
    return out
```

```python
from contextlib import ExitStack

import concourse.bass as bass
from concourse import mybir

ALU = mybir.AluOpType
ACT = mybir.ActivationFunctionType
F32 = mybir.dt.float32
F32R = mybir.dt.float32r
I32 = mybir.dt.int32
ds = bass.ds

P = 128
DEPTH = 2
T = 512
DM = 1024
KC = DM // P
D_CONV = 512
CC = D_CONV // P
TAPS = 31
NH = 4
D_FF = 2816
FC = D_FF // P
FTAPS = 3
PLE = 256
PC = PLE // P
EPS = 1e-6

TILE = P
UNIT = KC * TILE
PAIR = 2 * UNIT
HALF_DOWN = FC // 2 * TILE

PA, PB, PC_, PD, PE_, PF, PG, NPAIR = 0, 4, 12, 16, 38, 54, 56, 60
UA, UB, UC, UD, UE, UF, UG, NUNIT = 0, 8, 24, 32, 76, 84, 92, 100
WA_PAIRS = 42

G_MIX_PRE, G_MIX_POST, G_FFN_PRE, G_FFN_POST = 0, 8, 16, 24
CONV_W = 32
CONV_B = CONV_W + CC * TAPS
LN_G, LN_B, GN_G = CONV_B + 4, CONV_B + 8, CONV_B + 12
FW = CONV_B + 16
FB = FW + 2 * FC * FTAPS
NPAR = FB + 2 * FC

C_CENTER = 0
C_INVF, C_SIGN = C_CENTER + P, C_CENTER + P + 1
NCONST = C_SIGN + 1

TWO_PI_A, TWO_PI_B, TWO_PI_C = 6.28125, 0.0019350051879882812, 3.0199e-07
ROUND_MAGIC = 12582912.0
BIG_TURNS = 2.0 ** 15

START = 1


def build(nc, xT, pT, pos, masks, consts, params, wa, wd, wp, out):
    with ExitStack() as ctx:
        def sb(name, shape, dt=F32, stack=ctx):
            return stack.enter_context(nc.sbuf_tensor(name, shape, dt))

        def sem(name):
            return ctx.enter_context(nc.semaphore(name))

        x = sb("x", [P, KC * T])
        h_hi, h_lo = sb("h_hi", [P, KC * T], F32R), sb("h_lo", [P, KC * T], F32R)
        mT = sb("mT", [P, KC * T])
        raw = [sb(f"raw{s}", [P, PAIR]) for s in range(2)]
        w_hi = [sb(f"w_hi{s}", [P, PAIR], F32R) for s in range(2)]
        w_lo = [sb(f"w_lo{s}", [P, PAIR], F32R) for s in range(2)]
        cosT, sinT = sb("cosT", [P, T]), sb("sinT", [P, T])
        cst = sb("cst", [P, NCONST])
        par = sb("par", [P, DEPTH * NPAR])
        ones = sb("ones", [P, P])
        eps = sb("eps", [P, 1])
        half_pi = sb("half_pi", [P, 1])
        sumsq = sb("sumsq", [P, T])
        sq = [sb(f"sq{s}", [P, T]) for s in range(2)]
        std, rstd = sb("std", [P, T]), sb("rstd", [P, T])
        hx = [sb(f"hx{s}", [P, T]) for s in range(2)]
        positions = mT[:, 0:T].bitcast(I32)
        tap_gate, tap_value, gelu, hidden = (mT[:, n * T:(n + 1) * T] for n in range(4))
        praw = mT[:, (KC - PC) * T:KC * T]

        with ExitStack() as mixer:
            cat_hi = sb("cat_hi", [P, KC * T], F32R, mixer)
            cat_lo = sb("cat_lo", [P, KC * T], F32R, mixer)
            u = sb("u", [P, CC * T], F32, mixer)
            yc = sb("yc", [P, CC * T], F32, mixer)
            y_odd = sb("y_odd", [P, T], F32, mixer)
            sig = [sb(f"sig{s}", [P, T], F32, mixer) for s in range(2)]
            swp = [sb(f"swp{s}", [P, T], F32, mixer) for s in range(2)]
            tqk = sb("tqk", [P, T], F32, mixer)
            rot = [sb(f"rot{s}", [P, T], F32, mixer) for s in range(2)]
            vT = sb("vT", [P, T], F32, mixer)
            vc = sb("vc", [P, T], F32, mixer)
            silu_g = sb("silu_g", [P, T], F32, mixer)
            probs = [sb(f"probs{j}", [P, T - j * P], F32, mixer) for j in range(NH)]
            osq = sb("osq", [P, T], F32, mixer)
            mask = sb("mask", [P, NH * T], F32, mixer)
        with ExitStack() as mlp:
            a_hi = sb("a_hi", [P, FC * T], F32R, mlp)
            a_lo = sb("a_lo", [P, FC * T], F32R, mlp)
        with ExitStack() as embed:
            pw = sb("pw", [P, KC * T], F32, embed)
            gate = [sb(f"gate{s}", [P, T], F32, embed) for s in range(2)]
        sb("region", [P, 2 * FC * T])

        bank = [ctx.enter_context(nc.psum_tensor(f"bank{b}", [P, T], F32)) for b in range(8)]
        S_BANK, CV_BANK, O_BANK = (4, 5), 6, 7
        POST_BANK, PRE_BANK = 4, 5

        load_x, load_pos, load_cst, load_par = sem("load_x"), sem("load_pos"), sem("load_cst"), sem("load_par")
        load_mask = sem("load_mask")
        raw_full = [sem(f"raw_full{s}") for s in range(2)]
        p_full = sem("p_full")
        out_done = sem("out_done")
        ones_set = sem("ones_set")
        pos_f, red_r, abs_r = sem("pos_f"), sem("red_r"), sem("abs_r")
        trig = sem("trig")
        hi_ready, lo_ready = sem("hi_ready"), sem("lo_ready")
        half_done = sem("half_done")
        unit_ready = sem("unit_ready")
        hx_ready, hhi_ready, h_ready = sem("hx_ready"), sem("hhi_ready"), sem("h_ready")
        sig_ready, u_ready = sem("sig_ready"), sem("u_ready")
        swap_ready, qk_read, rot_ready = sem("swap_ready"), sem("qk_read"), sem("rot_ready")
        vt_ready, silu_ready = sem("vt_ready"), sem("silu_ready")
        scores_ready, probs_ready = sem("scores_ready"), sem("probs_ready")
        vc_done, vc_ready, o_done = sem("vc_done"), sem("vc_ready"), sem("o_done")
        osq_ready, ovar_done, ostd_ready, o_read = sem("osq_ready"), sem("ovar_done"), sem("ostd_ready"), sem("o_read")
        cat_ready = sem("cat_ready")
        conv_done, mean_done, cent_ready = sem("conv_done"), sem("mean_done"), sem("cent_ready")
        lnsq_ready, lnsq_used, lnstd_ready = sem("lnsq_ready"), sem("lnsq_used"), sem("lnstd_ready")
        norm_ready, lnact_ready, lncat_ready = sem("norm_ready"), sem("lnact_ready"), sem("lncat_ready")
        sq_ready, sq_added = sem("sq_ready"), sem("sq_added")
        m_ready = sem("m_ready")
        post_stat, post_std = sem("post_stat"), sem("post_std")
        x_new, xsq_ready, xsq_used, x_hi_ready = sem("x_new"), sem("xsq_ready"), sem("xsq_used"), sem("x_hi_ready")
        pre_stat, pre_std = sem("pre_stat"), sem("pre_std")
        tap_ready, conv3_ready, gelu_ready, a_ready = sem("tap_ready"), sem("conv3_ready"), sem("gelu_ready"), sem("a_ready")
        p_hi_ready, p_ready, pw_ready = sem("p_hi_ready"), sem("p_ready"), sem("pw_ready")
        gate_ready, xg_new = sem("gate_ready"), sem("xg_new")

        block = ctx.enter_context(nc.Block())
        ck = lambda c: slice(c * T, (c + 1) * T)

        def col(L, c, dyn=0):
            return par[:, ds(L * NPAR + c + dyn, 1)]

        @block.sync
        def _(sp):
            wa_r = wa.rearrange("l n p c -> (l n) p c")
            wd_r = wd.rearrange("l n p c -> (l n) p c")
            wp_r = wp.rearrange("l n p c -> (l n) p c")

            def load(L, base, i, s, src, row, width):
                sp.wait_ge(lo_ready, L * (2 * NPAIR) + i * 4 + (2 * (base + s) + 2))
                sp.dma_start(raw[s][:, 0:width], src[ds(row, 1), :, :].rearrange("a p c -> p (a c)")).then_inc(raw_full[s], 16)

            with sp.Fori(0, DEPTH) as L:
                sp.wait_ge(unit_ready, L * NUNIT + START)
                sp.dma_start(mask[:], masks).then_inc(load_mask, 16)
                with sp.Fori(0, PE_ // 2) as i:
                    for s in range(2):
                        load(L, 0, i, s, wa_r, L * WA_PAIRS + i * 2 + s, PAIR)
                sp.wait_ge(x_new, L * (2 * KC) + KC)
                sp.dma_start(praw.rearrange("p (k t) -> p k t", k=PC),
                             pT[ds(L, 1), :, :, :].rearrange("a k p t -> p (a k) t")).then_inc(p_full, 16)
                with sp.Fori(0, KC) as i:
                    for s in range(2):
                        load(L, PE_, i, s, wd_r, (L * KC + i) * 2 + s, HALF_DOWN)
                for s in range(2):
                    load(L, PF, 0, s, wp_r, L * 2 + s, UNIT)
                with sp.Fori(0, 2) as i:
                    for s in range(2):
                        load(L, PG, i, s, wa_r, L * WA_PAIRS + i * 2 + (PE_ + s), PAIR)
            for c in range(KC):
                sp.wait_ge(xg_new, KC * (DEPTH - 1) + c + 1)
                sp.dma_start(out[c], x[:, ck(c)]).then_inc(out_done, 16)
            sp.wait_ge(out_done, 16 * KC)

        @block.gpsimd
        def _(pool):
            pool.memset(ones[:], 1.0).then_inc(ones_set, 1)
            pool.memset(eps[:], EPS).then_inc(ones_set, 1)
            pool.memset(half_pi[:], 1.5707963267948966).then_inc(ones_set, 1)

        @block.tensor
        def _(pe):
            def tri(dst, whi, wlo, rhi, rlo, first, last):
                pe.matmul(dst, whi, rhi, start=first, stop=False)
                pe.matmul(dst, whi, rlo, start=False, stop=False)
                return pe.matmul(dst, wlo, rhi, start=False, stop=last)

            def tile_of(s, t):
                return w_hi[s][:, t * TILE:(t + 1) * TILE], w_lo[s][:, t * TILE:(t + 1) * TILE]

            def weights(L, base, i, s, half):
                pe.wait_ge(lo_ready, L * (2 * NPAIR) + i * 4 + (4 + 2 * (base + s) + half + 1))

            def project_unit(s, half, b, rhi, rlo):
                for k in range(KC):
                    last = tri(bank[b][:], *tile_of(s, half * KC + k), rhi[:, ck(k)], rlo[:, ck(k)], k == 0, k == KC - 1)
                return last.then_inc(unit_ready, 1)

            def project_pair_as_inputs_come(s, b, rhi, rlo, order, wait_input):
                for n, k in enumerate(order):
                    wait_input(n)
                    for half in range(2):
                        last = tri(bank[b + half][:], *tile_of(s, half * KC + k), rhi[:, ck(k)], rlo[:, ck(k)],
                                   n == 0, n == KC - 1)
                        if n == KC - 1:
                            last.then_inc(unit_ready, 1)

            def stat_of_sum(L, count, b, signal):
                pe.wait_ge(sq_added, count)
                pe.matmul(bank[b][:], ones[:], sumsq[:], start=True, stop=True).then_inc(signal, 1)

            pe.sem_inc(unit_ready, START)
            pe.sem_inc(scores_ready, START)
            pe.sem_inc(vc_done, START)
            pe.sem_inc(o_done, START)
            pe.wait_ge(ones_set, 3)
            pe.wait_ge(load_cst, 16)
            with pe.Fori(0, DEPTH) as L:
                stat_of_sum(L, L * (3 * KC) + KC, PRE_BANK, pre_stat)

                for p in range(4):
                    s = p % 2
                    weights(L, PA, 0, 0, 2 * p)
                    weights(L, PA, 0, 0, 2 * p + 1)
                    if p == 0:
                        pe.wait_ge(gate_ready, L * KC + START)
                        project_pair_as_inputs_come(s, 0, h_hi, h_lo, range(KC),
                                                    lambda n: pe.wait_ge(h_ready, L * (3 * KC) + (n + 1)))
                    else:
                        if p >= 2:
                            pe.wait_ge(u_ready, L * CC + (p - 1) + START)
                        project_unit(s, 0, 2 * s, h_hi, h_lo)
                        if p >= 2:
                            pe.wait_ge(sig_ready, L * CC + (p - 1))
                        project_unit(s, 1, 2 * s + 1, h_hi, h_lo)

                with pe.Fori(0, NH) as h:
                    pe.wait_ge(u_ready, L * CC + CC + START)
                    weights(L, PB, h, 0, 0)
                    pe.wait_ge(qk_read, L * (2 * NH) + h * 2 + START)
                    project_unit(0, 0, 0, h_hi, h_lo)
                    weights(L, PB, h, 0, 1)
                    project_unit(0, 1, 1, h_hi, h_lo)
                    weights(L, PB, h, 1, 0)
                    pe.wait_ge(vt_ready, L * NH + h + START)
                    project_unit(1, 0, 2, h_hi, h_lo)
                    pe.wait_ge(rot_ready, L * (2 * NH) + h * 2 + 2 + START)
                    for j in range(NH):
                        pe.wait_ge(probs_ready, L * (NH * NH) + h * NH + max(j - 1, 0) + START)
                        if j == 0:
                            pe.wait_ge(ostd_ready, L * NH + h + START)
                        pe.matmul(bank[S_BANK[j % 2]][:, 0:T - j * P], rot[1][:, j * P:(j + 1) * P], rot[0][:, j * P:T],
                                  start=True, stop=True).then_inc(scores_ready, 1)
                    pe.wait_ge(vt_ready, L * NH + h + 1 + START)
                    for j in range(NH):
                        last = pe.matmul(bank[CV_BANK][:, j * P:(j + 1) * P], vT[:, j * P:(j + 1) * P],
                                         cst[:, C_CENTER:C_CENTER + P], start=(j == 0), stop=(j == NH - 1),
                                         skip_group_check=True)
                    last.then_inc(vc_done, 1)
                    weights(L, PB, h, 1, 1)
                    pe.wait_ge(silu_ready, L * NH + h + START)
                    project_unit(1, 1, 3, h_hi, h_lo)
                    pe.wait_ge(vc_ready, L * NH + h + 1)
                    pe.wait_ge(o_read, L * NH + h + START)
                    for j in range(NH):
                        pe.wait_ge(probs_ready, L * (NH * NH) + h * NH + (j + 1) + START)
                        last = pe.matmul(bank[O_BANK][:, j * P:T], vc[:, j * P:(j + 1) * P], probs[j][:],
                                         start=(j == 0), stop=(j == NH - 1), skip_group_check=True)
                    last.then_inc(o_done, 1)
                    pe.wait_ge(osq_ready, L * NH + h + 1)
                    pe.matmul(bank[CV_BANK][:], ones[:], osq[:], start=True, stop=True).then_inc(ovar_done, 1)

                pe.wait_ge(conv_done, L * CC + CC)
                for j in range(CC):
                    last = pe.matmul(bank[4][:], ones[:], yc[:, ck(j)], start=(j == 0), stop=(j == CC - 1))
                last.then_inc(mean_done, 1)
                for j in range(CC):
                    pe.wait_ge(lnsq_ready, L * CC + (j + 1))
                    last = pe.matmul(bank[5][:], ones[:], sq[j % 2][:], start=(j == 0), stop=(j == CC - 1))
                    last.then_inc(lnsq_used, 1)

                for p in range(4):
                    s = p % 2
                    weights(L, PC_, 0, 0, 2 * p)
                    weights(L, PC_, 0, 0, 2 * p + 1)
                    if p == 0:
                        pe.wait_ge(silu_ready, L * NH + NH + START)
                        project_pair_as_inputs_come(s, 0, cat_hi, cat_lo, [4, 5, 6, 7, 0, 1, 2, 3],
                                                    lambda n: pe.wait_ge(cat_ready, L * NH + NH + START) if n < NH else
                                                    pe.wait_ge(lncat_ready, L * CC + (n - NH + 1)))
                    else:
                        for half in range(2):
                            if p >= 2:
                                pe.wait_ge(m_ready, L * (2 * KC) + (2 * p - 3 + half))
                            project_unit(s, half, 2 * s + half, cat_hi, cat_lo)
                stat_of_sum(L, L * (3 * KC) + 2 * KC, POST_BANK, post_stat)

                for c in range(KC):
                    pe.wait_ge(xsq_ready, L * KC + (c + 1))
                    last = pe.matmul(bank[PRE_BANK][:], ones[:], sq[c % 2][:], start=(c == 0), stop=(c == KC - 1))
                    if c < KC - 1:
                        last.then_inc(xsq_used, 1)
                last.then_inc(pre_stat, 1)

                def up_pair(i, s, first):
                    weights(L, PD, i, s, 0)
                    weights(L, PD, i, s, 1)
                    if first:
                        project_pair_as_inputs_come(s, 2 * s, h_hi, h_lo, range(KC),
                                                    lambda n: pe.wait_ge(h_ready, L * (3 * KC) + (KC + n + 1)))
                    else:
                        for half in range(2):
                            project_unit(s, half, 2 * s + half, h_hi, h_lo)

                up_pair(0, 0, True)
                up_pair(0, 1, False)
                with pe.Fori(1, FC // 2) as i:
                    for s in range(2):
                        pe.wait_ge(conv3_ready, L * (2 * FC) + i * 4 + (2 * s - 2))
                        up_pair(i, s, False)

                with pe.Fori(0, 2) as i:
                    pe.wait_ge(conv3_ready, L * (2 * FC) + 2 * FC)
                    for q in range(4):
                        pe.wait_ge(m_ready, L * (2 * KC) + i * 4 + (KC + q - 3 if q else KC - 3))
                        for s in range(2):
                            pe.wait_ge(lo_ready, L * (2 * NPAIR) + i * 16 + (4 + 2 * (PE_ + 2 * q + s) + 2))
                            pe.wait_ge(a_ready, L * FC + FC // 2 * (s + 1) + START)
                            for t in range(FC // 2):
                                k = s * (FC // 2) + t
                                last = tri(bank[q][:], *tile_of(s, t), a_hi[:, ck(k)], a_lo[:, ck(k)], k == 0, k == FC - 1)
                            last.then_inc((half_done, unit_ready)[s], 1)
        
                for s in range(2):
                    weights(L, PF, 0, s, 1)
                    if s == 0:
                        pe.wait_ge(p_ready, L * PC + PC)
                    for q in range(4):
                        if s == 0:
                            pe.wait_ge(m_ready, L * (2 * KC) + (KC + 5 + q))
                        else:
                            pe.wait_ge(pw_ready, L * KC + (q + 1))
                        for k in range(PC):
                            last = tri(bank[q][:], *tile_of(s, q * PC + k), h_hi[:, ck(k)], h_lo[:, ck(k)], k == 0, k == PC - 1)
                        last.then_inc(unit_ready, 1)
                    if s == 0:
                        stat_of_sum(L, L * (3 * KC) + 3 * KC, POST_BANK, post_stat)

                for p in range(4):
                    s = p % 2
                    weights(L, PG, 0, 0, 2 * p)
                    weights(L, PG, 0, 0, 2 * p + 1)
                    if p == 0:
                        pe.wait_ge(pw_ready, L * KC + KC)
                        project_pair_as_inputs_come(s, 0, h_hi, h_lo, range(KC),
                                                    lambda n: pe.wait_ge(h_ready, L * (3 * KC) + (2 * KC + n + 1)))
                    else:
                        for half in range(2):
                            if p >= 2:
                                pe.wait_ge(gate_ready, L * KC + (2 * p - 3 + half) + START)
                            project_unit(s, half, 2 * s + half, h_hi, h_lo)

        @block.scalar
        def _(act):
            def split_hi(L, base, i):
                s = base % 2
                last = base - 2
                if base <= PE_:
                    act.wait_ge(unit_ready, L * NUNIT + i * 4 + max(2 * last + 2, 0) + START)
                elif last >= PG:
                    act.wait_ge(unit_ready, L * NUNIT + (UG + 2 * (last - PG + 1)) + START)
                elif last >= PF:
                    act.wait_ge(unit_ready, L * NUNIT + (UF + 4 * (last - PF + 1)) + START)
                elif (last - PE_) % 2 == 0:
                    act.wait_ge(half_done, L * KC + i + ((last - PE_) // 2 + 1))
                else:
                    act.wait_ge(unit_ready, L * NUNIT + i + (UE + (last - PE_ + 1) // 2) + START)
                act.wait_ge(raw_full[s], L * (16 * NPAIR // 2) + i * 16 + (16 * (base // 2 + 1)))
                for half in range(2):
                    c = slice(half * UNIT, (half + 1) * UNIT)
                    act.activation(w_hi[s][:, c], raw[s][:, c], ACT.Copy).then_inc(hi_ready, 1)

            def root(b, features, signal):
                act.activation(std[:], bank[b][:], ACT.Sqrt, scale=1.0 / features, bias=eps[:, 0:1]).then_inc(signal, 1)

            def split_h_hi(L, phase):
                for c in range(KC):
                    act.wait_ge(hx_ready, L * (2 * KC) + (phase * KC + c + 1))
                    act.activation(h_hi[:, ck(c)], hx[c % 2][:], ACT.Copy).then_inc(hhi_ready, 1)

            def evacuate_m(L, n_unit, count, gain, dyn, b):
                act.wait_ge(unit_ready, n_unit + START)
                act.wait_ge(sq_added, count)
                act.activation(sq[b % 2][:], bank[b][:], ACT.Square).then_inc(sq_ready, 1)
                act.activation(mT[:, ds(dyn * T + b * T, T)], bank[b][:], ACT.Copy, scale=col(L, gain + b, dyn)).then_inc(m_ready, 1)

            act.dma_start(x[:].rearrange("p (c t) -> p c t", c=KC), xT.rearrange("c p t -> p c t")).then_inc(load_x, 16)
            act.dma_start(cst[:], consts).then_inc(load_cst, 16)
            act.dma_start(par[:], params).then_inc(load_par, 16)
            act.dma_start(positions, pos.broadcast_to([P, T])).then_inc(load_pos, 16)
            act.sem_inc(gate_ready, START)
            act.sem_inc(vt_ready, START)
            act.sem_inc(ostd_ready, START)
            act.sem_inc(silu_ready, START)
            act.wait_ge(load_x, 16)
            act.wait_ge(ones_set, 3)
            act.wait_ge(load_par, 16)
            act.wait_ge(load_cst, 16)
            for c in range(KC):
                if c >= 2:
                    act.wait_ge(sq_added, c - 1)
                act.activation(sq[c % 2][:], x[:, ck(c)], ACT.Square).then_inc(sq_ready, 1)
            act.wait_ge(red_r, 1)
            act.activation(std[:], hx[0][:], ACT.Abs).then_inc(abs_r, 1)
            act.activation(sinT[:], hx[0][:], ACT.Sin, scale=cst[:, C_SIGN:C_SIGN + 1]).then_inc(trig, 1)
            act.wait_ge(abs_r, 1)
            act.activation(cosT[:], std[:], ACT.Sin, scale=-1.0, bias=half_pi[:, 0:1]).then_inc(trig, 1)
            act.drain()

            with act.Fori(0, DEPTH) as L:
                split_hi(L, 0, 0)
                act.wait_ge(pre_stat, L * 2 + 1)
                root(PRE_BANK, DM, pre_std)
                split_h_hi(L, 0)

                for p in range(4):
                    split_hi(L, PA + p + 1, 0)
                    act.wait_ge(unit_ready, L * NUNIT + (UA + 2 * p + 2) + START)
                    if p >= 2:
                        act.wait_ge(u_ready, L * CC + (p - 1) + START)
                    act.activation(sig[p % 2][:], bank[2 * (p % 2) + 1][:], ACT.Sigmoid).then_inc(sig_ready, 1)

                with act.Fori(0, NH) as h:
                    split_hi(L, PB + 1, h)
                    for n in range(2):
                        act.wait_ge(unit_ready, L * NUNIT + h * 4 + (UB + n + 1) + START)
                        act.wait_ge(rot_ready, L * (2 * NH) + h * 2 + START)
                        act.activation(swp[n][0:64, :], bank[n][64:128, :], ACT.Copy)
                        act.activation(swp[n][64:128, :], bank[n][0:64, :], ACT.Copy).then_inc(swap_ready, 1)
                    split_hi(L, PB + 2, h)
                    act.wait_ge(unit_ready, L * NUNIT + h * 4 + (UB + 3) + START)
                    act.wait_ge(vc_done, L * NH + h + START)
                    act.activation(vT[:], bank[2][:], ACT.Copy).then_inc(vt_ready, 1)
                    act.wait_ge(vc_done, L * NH + h + 1 + START)
                    act.wait_ge(o_done, L * NH + h + START)
                    act.activation(vc[:], bank[CV_BANK][:], ACT.Copy).then_inc(vc_ready, 1)
                    act.wait_ge(unit_ready, L * NUNIT + h * 4 + (UB + 4) + START)
                    act.wait_ge(cat_ready, L * NH + h + START)
                    act.activation(silu_g[:], bank[3][:], ACT.Silu).then_inc(silu_ready, 1)
                    act.wait_ge(o_done, L * NH + h + 1 + START)
                    act.activation(osq[:], bank[O_BANK][:], ACT.Square).then_inc(osq_ready, 1)
                    act.wait_ge(ovar_done, L * NH + h + 1)
                    root(CV_BANK, P, ostd_ready)

                for j in range(CC):
                    act.wait_ge(cent_ready, L * CC + (j + 1))
                    if j >= 2:
                        act.wait_ge(lnsq_used, L * CC + (j - 1))
                    act.activation(sq[j % 2][:], yc[:, ck(j)], ACT.Square).then_inc(lnsq_ready, 1)
                act.wait_ge(lnsq_used, L * CC + CC)
                root(5, D_CONV, lnstd_ready)
                for j in range(CC):
                    act.wait_ge(norm_ready, L * CC + (j + 1))
                    act.activation(u[:, ck(j)], yc[:, ck(j)], ACT.Silu, scale=col(L, LN_G + j), bias=col(L, LN_B + j)).then_inc(lnact_ready, 1)

                with act.Fori(0, 2) as i:
                    for q in range(4):
                        if q % 2 == 0:
                            split_hi(L, PC_ + 1 + q // 2, i)
                        evacuate_m(L, L * NUNIT + i * 4 + (UC + q + 1), L * (3 * KC) + i * 4 + (KC + max(q - 1, 0)),
                                   G_MIX_POST, i * 4, q)

                act.wait_ge(post_stat, L * 2 + 1)
                root(POST_BANK, DM, post_std)
                for c in range(KC):
                    act.wait_ge(x_new, L * (2 * KC) + (c + 1))
                    if c >= 2:
                        act.wait_ge(xsq_used, L * (KC - 1) + (c - 1))
                    act.activation(sq[c % 2][:], x[:, ck(c)], ACT.Square).then_inc(xsq_ready, 1)
                act.wait_ge(pre_stat, L * 2 + 2)
                root(PRE_BANK, DM, pre_std)
                split_h_hi(L, 1)

                with act.Fori(0, FC // 2) as i:
                    for s in range(2):
                        split_hi(L, PD + 1 + s, i)
                        for n in range(2):
                            dst = (tap_gate, tap_value)[n]
                            act.wait_ge(unit_ready, L * NUNIT + i * 4 + (UD + 2 * s + n + 1) + START)
                            act.wait_ge(a_ready, L * FC + i * 2 + s + START)
                            uc = 2 * s + n
                            act.activation(dst, bank[uc][:], ACT.Identity,
                                           scale=col(L, FW + uc * FTAPS + 2, i * (4 * FTAPS)),
                                           bias=col(L, FB + uc, i * 4)).then_inc(tap_ready, 1)
                        act.wait_ge(conv3_ready, L * (2 * FC) + i * 4 + (2 * s + 1))
                        act.activation(gelu, tap_gate, ACT.Gelu_apprx_tanh).then_inc(gelu_ready, 1)

                act.wait_ge(p_full, L * 16 + 16)
                act.wait_ge(unit_ready, L * NUNIT + UE + START)
                act.activation(h_hi[:, 0:PC * T], praw, ACT.Copy).then_inc(p_hi_ready, 1)
                with act.Fori(0, 2) as i:
                    for q in range(4):
                        split_hi(L, PE_ + 1 + 2 * q, i * 4)
                        split_hi(L, PE_ + 2 + 2 * q, i * 4)
                        evacuate_m(L, L * NUNIT + i * 4 + (UE + q + 1), L * (3 * KC) + i * 4 + (2 * KC + max(q - 1, 0)),
                                   G_FFN_POST, i * 4, q)

                split_hi(L, PF + 1, 0)
                for q in range(4):
                    act.wait_ge(unit_ready, L * NUNIT + (UF + q + 1) + START)
                    act.activation(pw[:, ck(q)], bank[q][:], ACT.Copy).then_inc(pw_ready, 1)
                act.wait_ge(post_stat, L * 2 + 2)
                root(POST_BANK, DM, post_std)
                split_hi(L, PF + 2, 0)
                for q in range(4):
                    act.wait_ge(unit_ready, L * NUNIT + (UF + q + 5) + START)
                    act.activation(pw[:, ck(4 + q)], bank[q][:], ACT.Copy).then_inc(pw_ready, 1)
                for c in range(KC):
                    act.wait_ge(x_new, L * (2 * KC) + (KC + c + 1))
                    act.activation(h_hi[:, ck(c)], x[:, ck(c)], ACT.Copy).then_inc(x_hi_ready, 1)

                def square_x(m):
                    act.wait_ge(xg_new, L * KC + (m + 1))
                    if m >= 2:
                        act.wait_ge(sq_added, L * (3 * KC) + (3 * KC + m - 1))
                    act.activation(sq[m % 2][:], x[:, ck(m)], ACT.Square).then_inc(sq_ready, 1)

                for m in range(KC):
                    if m % 2 == 0 and m < 6:
                        split_hi(L, PG + 1 + m // 2, 0)
                    act.wait_ge(unit_ready, L * NUNIT + (UG + m + 1) + START)
                    if m >= 2:
                        act.wait_ge(xg_new, L * KC + (m - 1))
                    act.activation(gate[m % 2][:], bank[m % 4][:], ACT.Sigmoid).then_inc(gate_ready, 1)
                    if m >= 1:
                        square_x(m - 1)
                square_x(KC - 1)

        @block.vector
        def _(dve):
            def split_lo(L, base, i, halves=(0, 1)):
                s = base % 2
                for half in halves:
                    c = slice(half * UNIT, (half + 1) * UNIT)
                    dve.wait_ge(hi_ready, L * (2 * NPAIR) + i * 4 + (2 * base + half + 1))
                    dve.tensor_tensor(w_lo[s][:, c], raw[s][:, c], w_hi[s][:, c].bitcast(F32), ALU.subtract).then_inc(lo_ready, 1)

            def add_square(b, count):
                dve.drain()
                dve.wait_ge(sq_ready, count)
                dve.tensor_tensor(sumsq[:], sumsq[:], sq[b][:], ALU.add).then_inc(sq_added, 1)

            def inverse(signal, count):
                dve.drain()
                dve.wait_ge(signal, count)
                dve.reciprocal(rstd[:], std[:])
                dve.drain()

            def split_h_lo(L, phase, c):
                dve.wait_ge(hhi_ready, L * (2 * KC) + (phase * KC + c + 1))
                dve.tensor_tensor(h_lo[:, ck(c)], hx[c % 2][:], h_hi[:, ck(c)].bitcast(F32), ALU.subtract).then_inc(h_ready, 1)

            def make_h(L, phase, gain):
                for c in range(KC):
                    dve.scalar_tensor_tensor(out=hx[c % 2][:], in0=x[:, ck(c)], scalar=col(L, gain + c), in1=rstd[:],
                                             op0=ALU.mult, op1=ALU.mult).then_inc(hx_ready, 1)
                    if c >= 1:
                        split_h_lo(L, phase, c - 1)
                    dve.drain()
                split_h_lo(L, phase, KC - 1)

            def conv_steps(L, jd, steps):
                yj, cw = jd * T, jd * TAPS
                for n in steps:
                    dve.drain()
                    if n == TAPS // 2 + 1:
                        dve.tensor_tensor(yc[:, ds(yj, T)], yc[:, ds(yj, T)], y_odd[:], ALU.add).then_inc(conv_done, 1)
                        continue
                    for d in (2 * n, 2 * n + 1):
                        if d >= TAPS:
                            continue
                        w = col(L, CONV_W + TAPS - 1 - d, cw)
                        src = u[:, ds(yj, T - d)]
                        if d == 0:
                            dve.tensor_scalar(yc[:, ds(yj, T)], src, w, col(L, CONV_B, jd), ALU.mult, ALU.add)
                        elif d == 1:
                            dve.tensor_scalar(y_odd[:, 1:T], src, w, None, ALU.mult)
                        elif d % 2 == 0:
                            o = yc[:, ds(yj + d, T - d)]
                            dve.scalar_tensor_tensor(out=o, in0=src, scalar=w, in1=o, op0=ALU.mult, op1=ALU.add)
                        else:
                            o = y_odd[:, d:T]
                            dve.scalar_tensor_tensor(out=o, in0=src, scalar=w, in1=o, op0=ALU.mult, op1=ALU.add)

            dve.sem_inc(u_ready, START)
            dve.sem_inc(qk_read, START)
            dve.sem_inc(probs_ready, START)
            dve.sem_inc(o_read, START)
            dve.sem_inc(rot_ready, START)
            dve.sem_inc(cat_ready, START)
            dve.sem_inc(a_ready, START)
            dve.sem_inc(lo_ready, 4)
            dve.memset(sumsq[:], 0.0)
            for c in range(KC):
                add_square(c % 2, c + 1)
            dve.wait_ge(load_pos, 16)
            dve.wait_ge(load_cst, 16)
            dve.tensor_copy(hx[0][:], positions)
            dve.drain()
            dve.tensor_scalar(hx[0][:], hx[0][:], cst[:, C_INVF:C_INVF + 1], None, ALU.mult)
            two_pi = 6.283185307179586
            for turn in (BIG_TURNS, 1.0):
                dve.drain()
                dve.tensor_scalar(hx[1][:], hx[0][:], 1.0 / (two_pi * turn), ROUND_MAGIC, ALU.mult, ALU.add)
                dve.drain()
                dve.tensor_scalar(hx[1][:], hx[1][:], -ROUND_MAGIC, None, ALU.add)
                for part in (TWO_PI_A, TWO_PI_B, TWO_PI_C):
                    dve.drain()
                    dve.scalar_tensor_tensor(out=hx[0][:], in0=hx[1][:], scalar=-part * turn, in1=hx[0][:],
                                             op0=ALU.mult, op1=ALU.add)
            dve.drain()
            dve.tensor_scalar(hx[0][:], hx[0][:], 3.1415925, -3.1415925, ALU.min, ALU.max).then_inc(red_r, 1)
            dve.wait_ge(trig, 2)
            dve.wait_ge(load_par, 16)

            with dve.Fori(0, DEPTH) as L:
                split_lo(L, 0, 0)
                inverse(pre_std, L * 2 + 1)
                dve.memset(sumsq[:], 0.0)
                dve.memset(y_odd[:, 0:1], 0.0)
                make_h(L, 0, G_MIX_PRE)

                for p in range(4):
                    split_lo(L, PA + p + 1, 0)
                    dve.wait_ge(sig_ready, L * CC + (p + 1))
                    dve.tensor_tensor(u[:, ck(p)], bank[2 * (p % 2)][:], sig[p % 2][:], ALU.mult).then_inc(u_ready, 1)

                with dve.Fori(0, NH) as h:
                    conv_steps(L, h, range(0, 4))
                    split_lo(L, PB + 1, h)
                    for n in range(2):
                        dve.drain()
                        dve.wait_ge(swap_ready, L * (2 * NH) + h * 2 + (n + 1))
                        dve.tensor_tensor(tqk[:], bank[n][:], cosT[:], ALU.mult).then_inc(qk_read, 1)
                        dve.tensor_tensor(swp[n][:], swp[n][:], sinT[:], ALU.mult)
                        dve.drain()
                        dve.wait_ge(scores_ready, L * (NH * NH) + h * NH + START)
                        dve.tensor_tensor(rot[n][:], tqk[:], swp[n][:], ALU.add).then_inc(rot_ready, 1)
                        if n == 0:
                            conv_steps(L, h, range(4, 7))
                    conv_steps(L, h, range(7, 9))
                    split_lo(L, PB + 2, h)
                    dve.wait_ge(o_done, L * NH + h + START)
                    dve.wait_ge(load_mask, L * 16 + 16)
                    for j in range(NH):
                        dve.wait_ge(scores_ready, L * (NH * NH) + h * NH + (j + 1) + START)
                        dve.tensor_tensor(probs[j][:], bank[S_BANK[j % 2]][:, 0:T - j * P],
                                          mask[:, ds(h * T, T - j * P)], ALU.mult).then_inc(probs_ready, 1)
                    conv_steps(L, h, range(9, TAPS // 2 + 2))
                    inverse(ostd_ready, L * NH + h + 1 + START)
                    dve.scalar_tensor_tensor(out=hx[0][:], in0=bank[O_BANK][:], scalar=col(L, GN_G, h), in1=rstd[:],
                                             op0=ALU.mult, op1=ALU.mult).then_inc(o_read, 1)
                    dve.drain()
                    dve.wait_ge(silu_ready, L * NH + h + 1 + START)
                    dve.tensor_tensor(hx[1][:], hx[0][:], silu_g[:], ALU.mult)
                    dve.drain()
                    dve.tensor_copy(cat_hi[:, ds(h * T + CC * T, T)], hx[1][:])
                    dve.drain()
                    dve.tensor_tensor(cat_lo[:, ds(h * T + CC * T, T)], hx[1][:],
                                      cat_hi[:, ds(h * T + CC * T, T)].bitcast(F32), ALU.subtract).then_inc(cat_ready, 1)

                dve.wait_ge(mean_done, L + 1)
                for j in range(CC):
                    dve.scalar_tensor_tensor(out=yc[:, ck(j)], in0=bank[4][:], scalar=-1.0 / D_CONV, in1=yc[:, ck(j)],
                                             op0=ALU.mult, op1=ALU.add).then_inc(cent_ready, 1)
                inverse(lnstd_ready, L + 1)
                for j in range(CC):
                    dve.tensor_tensor(yc[:, ck(j)], yc[:, ck(j)], rstd[:], ALU.mult).then_inc(norm_ready, 1)
                for j in range(CC):
                    dve.wait_ge(lnact_ready, L * CC + (j + 1))
                    dve.tensor_copy(cat_hi[:, ck(j)], u[:, ck(j)])
                    dve.drain()
                    dve.tensor_tensor(cat_lo[:, ck(j)], u[:, ck(j)], cat_hi[:, ck(j)].bitcast(F32), ALU.subtract).then_inc(lncat_ready, 1)

                with dve.Fori(0, 2) as i:
                    for q in range(4):
                        if q % 2 == 0:
                            split_lo(L, PC_ + 1 + q // 2, i)
                        add_square(q % 2, L * (3 * KC) + i * 4 + (KC + q + 1))

                def update_x(L, phase):
                    inverse(post_std, L * 2 + (phase + 1))
                    dve.memset(sumsq[:], 0.0)
                    dve.wait_ge(m_ready, L * (2 * KC) + (phase + 1) * KC)
                    for c in range(KC + 1):
                        if c < KC:
                            dve.tensor_tensor(mT[:, ck(c)], mT[:, ck(c)], rstd[:], ALU.mult)
                        if c >= 1:
                            dve.tensor_tensor(x[:, ck(c - 1)], x[:, ck(c - 1)], mT[:, ck(c - 1)], ALU.add).then_inc(x_new, 1)
                        dve.drain()

                update_x(L, 0)
                inverse(pre_std, L * 2 + 2)
                make_h(L, 1, G_FFN_PRE)

                with dve.Fori(0, FC // 2) as i:
                    for s in range(2):
                        split_lo(L, PD + 1 + s, i)
                        for n in range(2):
                            dst, uc = (tap_gate, tap_value)[n], 2 * s + n
                            dve.wait_ge(tap_ready, L * (2 * FC) + i * 4 + (uc + 1))
                            for back in (1, 2):
                                ins = dve.scalar_tensor_tensor(
                                    out=dst[:, back:T], in0=bank[uc][:, 0:T - back],
                                    scalar=col(L, FW + uc * FTAPS + 2 - back, i * (4 * FTAPS)),
                                    in1=dst[:, back:T], op0=ALU.mult, op1=ALU.add)
                                if back == 1:
                                    dve.drain()
                            ins.then_inc(conv3_ready, 1)
                        dve.drain()
                        dve.wait_ge(gelu_ready, L * FC + i * 2 + (s + 1))
                        dve.tensor_tensor(hidden, gelu, tap_value, ALU.mult)
                        dve.drain()
                        o = ds(i * (2 * T) + s * T, T)
                        dve.tensor_copy(a_hi[:, o], hidden)
                        dve.drain()
                        dve.tensor_tensor(a_lo[:, o], hidden, a_hi[:, o].bitcast(F32), ALU.subtract).then_inc(a_ready, 1)

                dve.wait_ge(p_hi_ready, L + 1)
                for k in range(PC):
                    dve.tensor_tensor(h_lo[:, ck(k)], praw[:, ck(k)], h_hi[:, ck(k)].bitcast(F32), ALU.subtract).then_inc(p_ready, 1)
                with dve.Fori(0, 2) as i:
                    for q in range(4):
                        split_lo(L, PE_ + 1 + 2 * q, i * 4)
                        split_lo(L, PE_ + 2 + 2 * q, i * 4)
                        add_square(q % 2, L * (3 * KC) + i * 4 + (2 * KC + q + 1))
                split_lo(L, PF + 1, 0)

                def x_lo(c):
                    dve.wait_ge(x_hi_ready, L * KC + (c + 1))
                    dve.tensor_tensor(h_lo[:, ck(c)], x[:, ck(c)], h_hi[:, ck(c)].bitcast(F32), ALU.subtract).then_inc(h_ready, 1)

                update_x(L, 1)
                split_lo(L, PF + 2, 0)
                for c in range(KC):
                    x_lo(c)

                for m in range(KC):
                    if m % 2 == 0 and m < 6:
                        split_lo(L, PG + 1 + m // 2, 0)
                    dve.wait_ge(gate_ready, L * KC + (m + 1) + START)
                    dve.wait_ge(pw_ready, L * KC + KC)
                    dve.tensor_tensor(gate[m % 2][:], gate[m % 2][:], pw[:, ck(m)], ALU.mult)
                    dve.drain()
                    dve.tensor_tensor(x[:, ck(m)], x[:, ck(m)], gate[m % 2][:], ALU.add).then_inc(xg_new, 1)
                    if m >= 1:
                        add_square((m - 1) % 2, L * (3 * KC) + (3 * KC + m))
                add_square((KC - 1) % 2, L * (3 * KC) + 4 * KC)


def kernel(**inputs):
    import numpy as np
    import concourse.bacc as bacc
    from concourse.bass_utils import run_bass_kernel_spmd

    f32 = np.float32
    a = {k: np.asarray(v) for k, v in inputs.items()}

    def tiles(w, cols):
        c = w[:, cols:cols + P]
        return c.reshape(-1, P, P).transpose(1, 0, 2).reshape(P, -1)

    def unit_pairs(units):
        return [np.concatenate(units[n:n + 2], axis=1) for n in range(0, len(units), 2)]

    wa, wd, wp = [], [], []
    for L in range(DEPTH):
        w_in, w_out, up, down = a["w_in"][L], a["w_out"][L], a["ffn_up"][L], a["ffn_down"][L]
        units = []
        for j in range(CC):
            units += [tiles(w_in, j * P), tiles(w_in, D_CONV + j * P)]
        for h in range(NH):
            units += [tiles(w_in, 2 * D_CONV + g * NH * P + h * P) for g in range(4)]
        units += [tiles(w_out, m * P) for m in range(KC)]
        for j in range(FC):
            units += [tiles(up, D_FF + j * P), tiles(up, j * P)]
        units += [tiles(a["ple_gate"][L], m * P) for m in range(KC)]
        wa.append(np.stack(unit_pairs(units)))
        wd.append(np.stack([tiles(down, m * P)[:, s * HALF_DOWN:(s + 1) * HALF_DOWN] for m in range(KC) for s in range(2)]))
        ple = [tiles(a["ple_proj"][L], m * P) for m in range(KC)]
        wp.append(np.stack([np.concatenate(ple[4 * s:4 * s + 4], axis=1) for s in range(2)]))

    def cols(v):
        return np.ascontiguousarray(v.reshape(-1, P).T)

    params = []
    for L in range(DEPTH):
        cw = a["conv_w"][L].T.reshape(CC, P, TAPS).transpose(1, 0, 2).reshape(P, -1)
        fw = a["ffn_conv_w"][L].T.reshape(2, FC, P, FTAPS)[::-1].transpose(2, 1, 0, 3).reshape(P, -1)
        fb = a["ffn_conv_b"][L].reshape(2, FC, P)[::-1].transpose(2, 1, 0).reshape(P, -1)
        params += [cols(a[n][L]) for n in ("norm_mix_pre", "norm_mix_post", "norm_ffn_pre", "norm_ffn_post")]
        params += [cw, cols(a["conv_b"][L]), cols(a["conv_ln_g"][L]), cols(a["conv_ln_b"][L]), cols(a["ret_gn_g"][L]), fw, fb]
    params = np.concatenate(params, axis=1)

    n, m = np.arange(T)[None, :], np.arange(P)[:, None]
    masks = [np.where(n >= m, np.exp(np.log1p(-(2.0 ** (-5.0 - h))) * np.maximum(n - m, 0)), 0.0) * P ** -0.5 for h in range(NH)]
    inv_freq = f32(10000.0) ** (-(np.arange(P // 2, dtype=f32) / f32(P // 2)))
    consts = np.concatenate([np.eye(P) - 1.0 / P, np.tile(inv_freq, 2)[:, None],
                                     np.repeat([-1.0, 1.0], P // 2)[:, None]], axis=1).astype(f32)

    arrays = {
        "xT": a["x"][0].T.reshape(KC, P, T),
        "pT": a["p"][:, 0].transpose(0, 2, 1).reshape(DEPTH, PC, P, T),
        "pos": a["positions"].reshape(1, T),
        "masks": np.concatenate(masks, axis=1).astype(f32), "consts": consts, "params": params,
        "wa": np.stack(wa), "wd": np.stack(wd), "wp": np.stack(wp),
    }
    arrays = {k: np.ascontiguousarray(v) for k, v in arrays.items()}
    nc = bacc.Bacc("TRN2", target_bir_lowering=False, num_devices=1, dynamic_dma_scratch_size=1024)
    aps = [nc.dram_tensor(k, v.shape, mybir.dt.from_np(v.dtype), kind="ExternalInput").ap() for k, v in arrays.items()]
    out = nc.dram_tensor("out", (KC, P, T), F32, kind="ExternalOutput").ap()
    build(nc, *aps, out)
    r = run_bass_kernel_spmd(nc, [arrays], core_ids=[0])
    y = r.results[0]["out"]
    return np.ascontiguousarray(y.reshape(DM, T).T)[None]
```

```python
from contextlib import ExitStack

import concourse.bass as bass
from concourse import mybir

ALU = mybir.AluOpType
ACT = mybir.ActivationFunctionType
F32 = mybir.dt.float32
F32R = mybir.dt.float32r
I32 = mybir.dt.int32
ds = bass.ds

P = 128
DEPTH = 2
T = 512
DM = 1024
KC = DM // P
D_CONV = 512
CC = D_CONV // P
TAPS = 31
NH = 4
D_FF = 2816
FC = D_FF // P
FTAPS = 3
PLE = 256
PC = PLE // P
EPS = 1e-6

TILE = P
UNIT = KC * TILE
PAIR = 2 * UNIT
HALF_DOWN = FC // 2 * TILE

PA, PB, PC_, PD, PE_, PF, PG, NPAIR = 0, 4, 12, 16, 38, 54, 56, 60
UA, UB, UC, UD, UE, UF, UG, NUNIT = 0, 8, 24, 32, 76, 84, 92, 100
WA_PAIRS = 42

G_MIX_PRE, G_MIX_POST, G_FFN_PRE, G_FFN_POST = 0, 8, 16, 24
CONV_W = 32
CONV_B = CONV_W + CC * TAPS
LN_G, LN_B, GN_G = CONV_B + 4, CONV_B + 8, CONV_B + 12
FW = CONV_B + 16
FB = FW + 2 * FC * FTAPS
NPAR = FB + 2 * FC

C_CENTER, C_IDENT = 0, P
C_INVF, C_SIGN = 2 * P, 2 * P + 1
NCONST = C_SIGN + 1

TWO_PI_A, TWO_PI_B, TWO_PI_C = 6.28125, 0.0019350051879882812, 3.0199e-07
ROUND_MAGIC = 12582912.0
BIG_TURNS = 2.0 ** 15

N_MIX_PRE, N_HEAD, N_LN, N_MIX_POST, N_FFN_PRE, N_FFN_POST, NSTAT = 0, 1, NH + 1, NH + 2, NH + 3, NH + 4, NH + 5
Q_MIX_PRE, Q_LN, Q_MIX_POST, Q_FFN_POST, Q_NEXT = KC - 1, KC, KC + CC, 2 * KC + CC, 3 * KC + CC
NSQ = Q_NEXT

TB = T // P
STEPS = TAPS // 2 + 1
HEAD_STEPS = 12

START = 1


def build(nc, xT, pT, pos, masks, consts, params, wa, wd, wp, out):
    with ExitStack() as ctx:
        def sb(name, shape, dt=F32, stack=ctx):
            return stack.enter_context(nc.sbuf_tensor(name, shape, dt))

        def sem(name):
            return ctx.enter_context(nc.semaphore(name))

        x = sb("x", [P, KC * T])
        h_hi, h_lo = sb("h_hi", [P, KC * T], F32R), sb("h_lo", [P, KC * T], F32R)
        mT = sb("mT", [P, KC * T])
        raw = [sb(f"raw{s}", [P, PAIR]) for s in range(2)]
        w_hi = [sb(f"w_hi{s}", [P, PAIR], F32R) for s in range(2)]
        w_lo = [sb(f"w_lo{s}", [P, PAIR], F32R) for s in range(2)]
        angle = sb("angle", [P, T])
        cosT, sinT = sb("cosT", [P, T]), sb("sinT", [P, T])
        cst = sb("cst", [P, NCONST])
        par = sb("par", [P, DEPTH * NPAR])
        ones = sb("ones", [P, P])
        eps = sb("eps", [P, 1])
        half_pi = sb("half_pi", [P, 1])
        sumsq = sb("sumsq", [P, T])
        sq = [sb(f"sq{s}", [P, T]) for s in range(2)]
        std_tok, rstd_tok = sb("std_tok", [P, TB]), sb("rstd_tok", [P, TB])
        junk = sb("junk", [P, 4])
        hx = [sb(f"hx{s}", [P, T]) for s in range(2)]
        positions = mT[:, 0:T].bitcast(I32)
        tap_gate, tap_value, gelu, hidden = (mT[:, n * T:(n + 1) * T] for n in range(4))
        praw = mT[:, (KC - PC) * T:KC * T]

        with ExitStack() as mixer:
            cat_hi = sb("cat_hi", [P, KC * T], F32R, mixer)
            cat_lo = sb("cat_lo", [P, KC * T], F32R, mixer)
            u = sb("u", [P, CC * T], F32, mixer)
            yc = sb("yc", [P, CC * T], F32, mixer)
            y_odd = sb("y_odd", [P, T], F32, mixer)
            sig = [sb(f"sig{s}", [P, T], F32, mixer) for s in range(2)]
            swp = [sb(f"swp{s}", [P, T], F32, mixer) for s in range(2)]
            tqk = sb("tqk", [P, T], F32, mixer)
            rot = [sb(f"rot{s}", [P, T], F32, mixer) for s in range(2)]
            vT = sb("vT", [P, T], F32, mixer)
            vc = sb("vc", [P, T], F32, mixer)
            silu_g = sb("silu_g", [P, T], F32, mixer)
            probs = [sb(f"probs{j}", [P, T - j * P], F32, mixer) for j in range(NH)]
            osq = sb("osq", [P, T], F32, mixer)
            turns = sb("turns", [P, T], F32, mixer)
            mask = sb("mask", [P, NH * T], F32, mixer)
        with ExitStack() as mlp:
            a_hi = sb("a_hi", [P, FC * T], F32R, mlp)
            a_lo = sb("a_lo", [P, FC * T], F32R, mlp)
        with ExitStack() as embed:
            pw = sb("pw", [P, KC * T], F32, embed)
            gate = [sb(f"gate{s}", [P, T], F32, embed) for s in range(2)]
        sb("region", [P, 2 * FC * T])

        bank = [ctx.enter_context(nc.psum_tensor(f"bank{b}", [P, T], F32)) for b in range(8)]
        S_BANK, CV_BANK, O_BANK = (4, 5), 6, 7
        POST_BANK, PRE_BANK = 4, 5

        load_x = [sem(f"load_x{c}") for c in range(KC)]
        load_pos, load_cst, load_par = sem("load_pos"), sem("load_cst"), sem("load_par")
        load_mask = sem("load_mask")
        raw_full = [sem(f"raw_full{s}") for s in range(2)]
        p_full = sem("p_full")
        out_done = sem("out_done")
        ones_set = sem("ones_set")
        angle_ready, trig_ready = sem("angle_ready"), sem("trig_ready")
        hi_ready, lo_ready = sem("hi_ready"), sem("lo_ready")
        half_done = sem("half_done")
        unit_ready = sem("unit_ready")
        hx_ready, hhi_ready, h_ready = sem("hx_ready"), sem("hhi_ready"), sem("h_ready")
        sig_ready, u_ready = sem("sig_ready"), sem("u_ready")
        swap_ready, qk_read, rot_ready = sem("swap_ready"), sem("qk_read"), sem("rot_ready")
        vt_ready, silu_ready = sem("vt_ready"), sem("silu_ready")
        scores_ready, probs_ready = sem("scores_ready"), sem("probs_ready")
        vc_done, vc_ready, o_done = sem("vc_done"), sem("vc_ready"), sem("o_done")
        osq_ready, o_read = sem("osq_ready"), sem("o_read")
        gn_ready, cat_hi_ready, cat_ready = sem("gn_ready"), sem("cat_hi_ready"), sem("cat_ready")
        conv_done, mean_done, cent_ready = sem("conv_done"), sem("mean_done"), sem("cent_ready")
        norm_ready, lnhi_ready, lncat_ready = sem("norm_ready"), sem("lnhi_ready"), sem("lncat_ready")
        sq_ready, sq_added = sem("sq_ready"), sem("sq_added")
        m_ready = sem("m_ready")
        sums_done, root_done = sem("sums_done"), sem("root_done")
        inverse_ready, spread_done = sem("inverse_ready"), sem("spread_done")
        x_new, xsq_ready, xsq_used, x_hi_ready = sem("x_new"), sem("xsq_ready"), sem("xsq_used"), sem("x_hi_ready")
        tap_ready, conv3_ready, gelu_ready, a_ready = sem("tap_ready"), sem("conv3_ready"), sem("gelu_ready"), sem("a_ready")
        p_hi_ready, p_ready, pw_ready = sem("p_hi_ready"), sem("p_ready"), sem("pw_ready")
        gate_ready, xg_new = sem("gate_ready"), sem("xg_new")

        block = ctx.enter_context(nc.Block())
        ck = lambda c: slice(c * T, (c + 1) * T)

        def col(L, c, dyn=0):
            return par[:, ds(L * NPAR + c + dyn, 1)]

        @block.sync
        def _(sp):
            wa_r = wa
            wd_r = wd.rearrange("l n p c -> (l n) p c")
            wp_r = wp.rearrange("l n p c -> (l n) p c")

            def load(L, base, i, s, src, row, width):
                sp.wait_ge(lo_ready, L * (2 * NPAIR) + i * 4 + (2 * (base + s) + 2))
                sp.dma_start(raw[s][:, 0:width], src[ds(row, 1), :, :].rearrange("a p c -> p (a c)")).then_inc(raw_full[s], 16)

            def load_a(L, n, i, s):
                load(L, n - s, i, s, wa_r, L * WA_PAIRS + i * 2 + n, PAIR)

            for c in range(KC // 2, KC):
                sp.dma_start(x[:, ck(c)], xT[c]).then_inc(load_x[c], 16)
            sp.dma_start(raw[0][:], wa_r[0]).then_inc(raw_full[0], 16)
            with sp.Fori(0, DEPTH) as L:
                load_a(L, 1, 0, 1)
                load_a(L, 2, 0, 0)
                load_a(L, 3, 0, 1)
                sp.wait_ge(unit_ready, L * NUNIT + START)
                sp.dma_start(mask[:], masks).then_inc(load_mask, 16)
                with sp.Fori(0, (PE_ - PB) // 2) as i:
                    for s in range(2):
                        load_a(L, PB + s, i, s)
                sp.wait_ge(x_new, L * (2 * KC) + KC)
                sp.dma_start(praw.rearrange("p (k t) -> p k t", k=PC),
                             pT[ds(L, 1), :, :, :].rearrange("a k p t -> p (a k) t")).then_inc(p_full, 16)
                with sp.Fori(0, KC) as i:
                    for s in range(2):
                        load(L, PE_, i, s, wd_r, (L * KC + i) * 2 + s, HALF_DOWN)
                for s in range(2):
                    load(L, PF, 0, s, wp_r, L * 2 + s, UNIT)
                with sp.Fori(0, 2) as i:
                    for s in range(2):
                        load(L, PG, i, s, wa_r, L * WA_PAIRS + i * 2 + (PE_ + s), PAIR)
                load(L, NPAIR, 0, 0, wa_r, L * WA_PAIRS + WA_PAIRS, PAIR)
            for c in range(KC):
                sp.wait_ge(xg_new, KC * (DEPTH - 1) + c + 1 + START)
                sp.dma_start(out[c], x[:, ck(c)]).then_inc(out_done, 16)
            sp.wait_ge(out_done, 16 * KC)

        @block.gpsimd
        def _(pool):
            pool.memset(ones[:], 1.0).then_inc(ones_set, 1)
            pool.memset(eps[:], EPS).then_inc(ones_set, 1)
            pool.memset(half_pi[:], 1.5707963267948966).then_inc(ones_set, 1)
            pool.wait_ge(load_pos, 16)
            pool.wait_ge(load_cst, 16)
            pool.tensor_copy(angle[:], positions)
            pool.drain()
            pool.tensor_scalar(angle[:], angle[:], cst[:, C_INVF:C_INVF + 1], None, ALU.mult)
            two_pi = 6.283185307179586
            for turn in (BIG_TURNS, 1.0):
                pool.drain()
                pool.tensor_scalar(turns[:], angle[:], 1.0 / (two_pi * turn), ROUND_MAGIC, ALU.mult, ALU.add)
                pool.drain()
                pool.tensor_scalar(turns[:], turns[:], -ROUND_MAGIC, None, ALU.add)
                for part in (TWO_PI_A, TWO_PI_B, TWO_PI_C):
                    pool.drain()
                    pool.tensor_scalar(tqk[:], turns[:], -part * turn, None, ALU.mult)
                    pool.drain()
                    pool.tensor_tensor(angle[:], angle[:], tqk[:], ALU.add)
            pool.drain()
            pool.tensor_scalar(angle[:], angle[:], 3.1415925, -3.1415925, ALU.min, ALU.max).then_inc(angle_ready, 1)

        @block.tensor
        def _(pe):
            def tri(dst, whi, wlo, rhi, rlo, first, last):
                pe.matmul(dst, whi, rhi, start=first, stop=False)
                pe.matmul(dst, whi, rlo, start=False, stop=False)
                return pe.matmul(dst, wlo, rhi, start=False, stop=last)

            def tile_of(s, t):
                return w_hi[s][:, t * TILE:(t + 1) * TILE], w_lo[s][:, t * TILE:(t + 1) * TILE]

            def weights(L, base, i, s, half):
                pe.wait_ge(lo_ready, L * (2 * NPAIR) + i * 4 + (4 + 2 * (base + s) + half + 1))

            def project_part(s, half, b, rhi, rlo, ks):
                for k in ks:
                    last = tri(bank[b][:], *tile_of(s, half * KC + k), rhi[:, ck(k)], rlo[:, ck(k)], k == 0, k == KC - 1)
                return last

            def project_unit(s, half, b, rhi, rlo):
                return project_part(s, half, b, rhi, rlo, range(KC)).then_inc(unit_ready, 1)

            def project_pair(s, b, rhi, rlo, order, wait_input, first=True, last=True):
                for n, k in enumerate(order):
                    wait_input(k)
                    for half in range(2):
                        end = last and n == len(order) - 1
                        ins = tri(bank[b + half][:], *tile_of(s, half * KC + k), rhi[:, ck(k)], rlo[:, ck(k)],
                                  first and n == 0, end)
                        if end:
                            ins.then_inc(unit_ready, 1)

            def token_sums(b, src, first=True, last=True):
                for j in range(TB):
                    ins = pe.matmul(bank[b][:, j:j + 1], src[:, j * P:(j + 1) * P], ones[:, 0:1],
                                    start=first and j == 0, stop=last and j == TB - 1, skip_group_check=True)
                return ins

            def sums_of_squares(L, count, b):
                pe.wait_ge(sq_added, L * NSQ + count)
                token_sums(b, sumsq).then_inc(sums_done, 1)

            def spread(L, n, b, dyn=0):
                pe.wait_ge(inverse_ready, L * NSTAT + dyn + (n + 1))
                for j in range(TB):
                    ins = pe.matmul(bank[b][:, j * P:(j + 1) * P], rstd_tok[:, j:j + 1].broadcast_to([P, P]),
                                    cst[:, C_IDENT:C_IDENT + P], start=(j == 0), stop=(j == TB - 1), skip_group_check=True)
                ins.then_inc(spread_done, 1)

            for signal in (unit_ready, scores_ready, vc_done, o_done):
                pe.sem_inc(signal, START)
            pe.wait_ge(ones_set, 3)
            pe.wait_ge(load_cst, 16)
            with pe.Fori(0, DEPTH) as L:
                sums_of_squares(L, Q_LN, PRE_BANK)
                spread(L, N_MIX_PRE, PRE_BANK)

                for p in range(4):
                    s = p % 2
                    weights(L, PA, 0, 0, 2 * p)
                    weights(L, PA, 0, 0, 2 * p + 1)
                    if p == 0:
                        pe.wait_ge(gate_ready, L * KC + START)
                        project_pair(s, 0, h_hi, h_lo, range(KC), lambda k: pe.wait_ge(h_ready, L * (3 * KC) + (k + 1)))
                    else:
                        if p >= 2:
                            pe.wait_ge(u_ready, L * CC + (p - 1) + START)
                        project_unit(s, 0, 2 * s, h_hi, h_lo)
                        if p >= 2:
                            pe.wait_ge(sig_ready, L * CC + (p - 1))
                        project_unit(s, 1, 2 * s + 1, h_hi, h_lo)

                with pe.Fori(0, NH) as h:
                    weights(L, PB, h, 0, 0)
                    pe.wait_ge(u_ready, L * CC + CC - 1 + START)
                    pe.wait_ge(qk_read, L * (2 * NH) + h * 2 + START)
                    project_unit(0, 0, 0, h_hi, h_lo)
                    weights(L, PB, h, 0, 1)
                    project_unit(0, 1, 1, h_hi, h_lo)
                    weights(L, PB, h, 1, 0)
                    pe.wait_ge(u_ready, L * CC + CC + START)
                    pe.wait_ge(vt_ready, L * NH + h + START)
                    project_unit(1, 0, 2, h_hi, h_lo)
                    pe.wait_ge(rot_ready, L * (2 * NH) + h * 2 + 2 + START)
                    for j in range(NH):
                        pe.wait_ge(probs_ready, L * (NH * NH) + h * NH + max(j - 1, 0) + START)
                        pe.matmul(bank[S_BANK[j % 2]][:, 0:T - j * P], rot[1][:, j * P:(j + 1) * P], rot[0][:, j * P:T],
                                  start=True, stop=True).then_inc(scores_ready, 1)
                    pe.wait_ge(vt_ready, L * NH + h + 1 + START)
                    pe.wait_ge(gn_ready, L * NH + h + START)
                    for j in range(NH):
                        last = pe.matmul(bank[CV_BANK][:, j * P:(j + 1) * P], vT[:, j * P:(j + 1) * P],
                                         cst[:, C_CENTER:C_CENTER + P], start=(j == 0), stop=(j == NH - 1),
                                         skip_group_check=True)
                    last.then_inc(vc_done, 1)
                    weights(L, PB, h, 1, 1)
                    pe.wait_ge(silu_ready, L * NH + h + START)
                    project_part(1, 1, 3, h_hi, h_lo, range(0, 3))
                    pe.wait_ge(vc_ready, L * NH + h + 1)
                    pe.wait_ge(o_read, L * NH + h + START)
                    for j in range(NH):
                        pe.wait_ge(probs_ready, L * (NH * NH) + h * NH + (j + 1) + START)
                        last = pe.matmul(bank[O_BANK][:, j * P:T], vc[:, j * P:(j + 1) * P], probs[j][:],
                                         start=(j == 0), stop=(j == NH - 1), skip_group_check=True)
                    last.then_inc(o_done, 1)
                    project_part(1, 1, 3, h_hi, h_lo, range(3, 5))
                    pe.wait_ge(osq_ready, L * NH + h + 1)
                    token_sums(CV_BANK, osq).then_inc(sums_done, 1)
                    project_part(1, 1, 3, h_hi, h_lo, range(5, KC)).then_inc(unit_ready, 1)
                    spread(L, N_HEAD, CV_BANK, h)

                pe.wait_ge(conv_done, L + 1)
                for j in range(CC):
                    last = pe.matmul(bank[4][:], ones[:], yc[:, ck(j)], start=(j == 0), stop=(j == CC - 1))
                last.then_inc(mean_done, 1)

                weights(L, PC_, 0, 0, 1)
                pe.wait_ge(silu_ready, L * NH + NH + START)
                heads, conv = range(CC, KC), range(CC)
                project_pair(0, 0, cat_hi, cat_lo, heads, lambda k: pe.wait_ge(cat_ready, L * NH + NH + START), last=False)
                sums_of_squares(L, Q_MIX_POST, 5)
                weights(L, PC_, 0, 0, 3)
                project_pair(1, 2, cat_hi, cat_lo, heads[:2], lambda k: None, last=False)
                spread(L, N_LN, 5)
                project_pair(1, 2, cat_hi, cat_lo, heads[2:], lambda k: None, first=False, last=False)
                for s in range(2):
                    project_pair(s, 2 * s, cat_hi, cat_lo, conv, lambda k: pe.wait_ge(lncat_ready, L * CC + (k + 1)), first=False)
                for s in range(2):
                    for half in range(2):
                        weights(L, PC_ + 2, 0, s, half)
                        pe.wait_ge(m_ready, L * (2 * KC) + (2 * s + half + 1))
                        project_unit(s, half, 2 * s + half, cat_hi, cat_lo)
                sums_of_squares(L, Q_FFN_POST, POST_BANK)
                spread(L, N_MIX_POST, POST_BANK)

                for c in range(KC):
                    pe.wait_ge(xsq_ready, L * KC + (c + 1))
                    last = token_sums(PRE_BANK, sq[c % 2], first=(c == 0), last=(c == KC - 1))
                    last.then_inc((xsq_used, sums_done)[c == KC - 1], 1)
                spread(L, N_FFN_PRE, PRE_BANK)

                def up_pair(i, s, first):
                    weights(L, PD, i, s, 0)
                    weights(L, PD, i, s, 1)
                    if first:
                        project_pair(s, 2 * s, h_hi, h_lo, range(KC),
                                     lambda k: pe.wait_ge(h_ready, L * (3 * KC) + (KC + k + 1)))
                    else:
                        for half in range(2):
                            project_unit(s, half, 2 * s + half, h_hi, h_lo)

                up_pair(0, 0, True)
                up_pair(0, 1, False)
                with pe.Fori(1, FC // 2) as i:
                    for s in range(2):
                        pe.wait_ge(conv3_ready, L * (2 * FC) + i * 4 + (2 * s - 2))
                        up_pair(i, s, False)

                with pe.Fori(0, 2) as i:
                    pe.wait_ge(conv3_ready, L * (2 * FC) + 2 * FC)
                    for q in range(4):
                        pe.wait_ge(m_ready, L * (2 * KC) + i * 4 + (KC + q - 3 if q else KC - 3))
                        for s in range(2):
                            pe.wait_ge(lo_ready, L * (2 * NPAIR) + i * 16 + (4 + 2 * (PE_ + 2 * q + s) + 2))
                            pe.wait_ge(a_ready, L * FC + FC // 2 * (s + 1) + START)
                            for t in range(FC // 2):
                                k = s * (FC // 2) + t
                                last = tri(bank[q][:], *tile_of(s, t), a_hi[:, ck(k)], a_lo[:, ck(k)], k == 0, k == FC - 1)
                            last.then_inc((half_done, unit_ready)[s], 1)
        
                for s in range(2):
                    weights(L, PF, 0, s, 1)
                    if s == 0:
                        pe.wait_ge(p_ready, L * PC + PC)
                    for q in range(4):
                        if s == 0:
                            pe.wait_ge(m_ready, L * (2 * KC) + (KC + 5 + q))
                        else:
                            pe.wait_ge(pw_ready, L * KC + (q + 1))
                        for k in range(PC):
                            c = KC - PC + k
                            last = tri(bank[q][:], *tile_of(s, q * PC + k), h_hi[:, ck(c)], h_lo[:, ck(c)], k == 0, k == PC - 1)
                        last.then_inc(unit_ready, 1)
                        if s == 0 and q == 1:
                            sums_of_squares(L, Q_NEXT, POST_BANK)
                    if s == 0:
                        spread(L, N_FFN_POST, POST_BANK)

                for p in range(4):
                    s = p % 2
                    weights(L, PG, 0, 0, 2 * p)
                    weights(L, PG, 0, 0, 2 * p + 1)
                    if p == 0:
                        pe.wait_ge(pw_ready, L * KC + KC - 2)
                        project_pair(s, 0, h_hi, h_lo, range(KC),
                                     lambda k: pe.wait_ge(h_ready, L * (3 * KC) + (2 * KC + k + 1)))
                    else:
                        for half in range(2):
                            if p == 1:
                                pe.wait_ge(pw_ready, L * KC + KC - 1 + half)
                            else:
                                pe.wait_ge(gate_ready, L * KC + (2 * p - 3 + half) + START)
                            project_unit(s, half, 2 * s + half, h_hi, h_lo)

        @block.scalar
        def _(act):
            def split_hi(L, base, i):
                s = base % 2
                last = base - 2
                if base <= PE_:
                    act.wait_ge(unit_ready, L * NUNIT + i * 4 + max(2 * last + 2, 0) + START)
                elif last >= PG:
                    act.wait_ge(unit_ready, L * NUNIT + (UG + 2 * (last - PG + 1)) + START)
                elif last >= PF:
                    act.wait_ge(unit_ready, L * NUNIT + (UF + 4 * (last - PF + 1)) + START)
                elif (last - PE_) % 2 == 0:
                    act.wait_ge(half_done, L * KC + i + ((last - PE_) // 2 + 1))
                else:
                    act.wait_ge(unit_ready, L * NUNIT + i + (UE + (last - PE_ + 1) // 2) + START)
                act.wait_ge(raw_full[s], L * (16 * NPAIR // 2) + i * 16 + (16 * (base // 2 + 1)))
                for half in range(2):
                    c = slice(half * UNIT, (half + 1) * UNIT)
                    act.activation(w_hi[s][:, c], raw[s][:, c], ACT.Copy).then_inc(hi_ready, 1)

            def load_table(func):
                act.activation(junk[:, 0:1], eps[:, 0:1], func)
                act.drain()

            def root(L, n, b, features, dyn=0):
                act.wait_ge(sums_done, L * NSTAT + dyn + (n + 1))
                act.activation(std_tok[:], bank[b][:, 0:TB], ACT.Sqrt, scale=1.0 / features, bias=eps[:, 0:1]).then_inc(root_done, 1)

            def split_h_hi(L, phase):
                for c in range(KC):
                    act.wait_ge(hx_ready, L * (2 * KC) + (phase * KC + c + 1))
                    act.activation(h_hi[:, ck(c)], hx[c % 2][:], ACT.Copy).then_inc(hhi_ready, 1)

            def evacuate_m(L, n_unit, n_sq, gain, dyn, b):
                act.wait_ge(unit_ready, n_unit + START)
                act.wait_ge(sq_added, n_sq - 1)
                act.activation(sq[b % 2][:], bank[b][:], ACT.Square).then_inc(sq_ready, 1)
                act.activation(mT[:, ds(dyn * T + b * T, T)], bank[b][:], ACT.Copy, scale=col(L, gain + b, dyn)).then_inc(m_ready, 1)

            for c in range(KC // 2):
                act.dma_start(x[:, ck(c)], xT[c]).then_inc(load_x[c], 16)
                if c == KC // 2 - 1:
                    act.dma_start(cst[:], consts).then_inc(load_cst, 16)
                    act.dma_start(positions, pos.broadcast_to([P, T])).then_inc(load_pos, 16)
            act.dma_start(par[:], params).then_inc(load_par, 16)
            for signal in (gate_ready, vt_ready, silu_ready):
                act.sem_inc(signal, START)
            act.wait_ge(ones_set, 3)
            for c in range(KC - 1):
                act.wait_ge(load_x[c], 16)
                if c >= 2:
                    act.wait_ge(sq_added, c - 1)
                act.activation(sq[c % 2][:], x[:, ck(c)], ACT.Square).then_inc(sq_ready, 1)
            split_hi(0, 0, 0)
            act.wait_ge(load_x[KC - 1], 16)
            act.wait_ge(load_par, 16)
            act.wait_ge(load_cst, 16)

            with act.Fori(0, DEPTH) as L:
                act.wait_ge(xg_new, L * KC + START)
                act.wait_ge(sq_added, L * NSQ + (Q_MIX_PRE - 1))
                act.activation(sq[Q_MIX_PRE % 2][:], x[:, ck(KC - 1)], ACT.Square).then_inc(sq_ready, 1)
                load_table(ACT.Sqrt)
                root(L, N_MIX_PRE, PRE_BANK, DM)
                split_h_hi(L, 0)

                for p in range(4):
                    split_hi(L, PA + p + 1, 0)
                    if p == 2:
                        act.wait_ge(angle_ready, 1)
                        act.activation(cosT[:], angle[:], ACT.Abs)
                        act.activation(sinT[:], angle[:], ACT.Sin, scale=cst[:, C_SIGN:C_SIGN + 1]).then_inc(trig_ready, 1)
                        act.drain()
                        act.activation(cosT[:], cosT[:], ACT.Sin, scale=-1.0, bias=half_pi[:, 0:1]).then_inc(trig_ready, 1)
                    load_table(ACT.Sigmoid)
                    act.wait_ge(unit_ready, L * NUNIT + (UA + 2 * p + 2) + START)
                    if p >= 2:
                        act.wait_ge(u_ready, L * CC + (p - 1) + START)
                    act.activation(sig[p % 2][:], bank[2 * (p % 2) + 1][:], ACT.Sigmoid).then_inc(sig_ready, 1)

                with act.Fori(0, NH) as h:
                    split_hi(L, PB + 1, h)
                    for n in range(2):
                        act.wait_ge(unit_ready, L * NUNIT + h * 4 + (UB + n + 1) + START)
                        act.wait_ge(rot_ready, L * (2 * NH) + h * 2 + START)
                        act.activation(swp[n][0:64, :], bank[n][64:128, :], ACT.Copy)
                        act.activation(swp[n][64:128, :], bank[n][0:64, :], ACT.Copy).then_inc(swap_ready, 1)
                    split_hi(L, PB + 2, h)
                    act.wait_ge(unit_ready, L * NUNIT + h * 4 + (UB + 3) + START)
                    act.wait_ge(vc_done, L * NH + h + START)
                    act.activation(vT[:], bank[2][:], ACT.Copy).then_inc(vt_ready, 1)
                    act.wait_ge(vc_done, L * NH + h + 1 + START)
                    act.wait_ge(o_done, L * NH + h + START)
                    act.activation(vc[:], bank[CV_BANK][:], ACT.Copy).then_inc(vc_ready, 1)
                    load_table(ACT.Sqrt)
                    act.wait_ge(o_done, L * NH + h + 1 + START)
                    act.activation(osq[:], bank[O_BANK][:], ACT.Square).then_inc(osq_ready, 1)
                    root(L, N_HEAD, CV_BANK, P, h)
                    load_table(ACT.Silu)
                    act.wait_ge(unit_ready, L * NUNIT + h * 4 + (UB + 4) + START)
                    act.wait_ge(o_read, L * NH + h + START)
                    act.activation(silu_g[:], bank[3][:], ACT.Silu).then_inc(silu_ready, 1)
                    act.wait_ge(gn_ready, L * NH + h + 1 + START)
                    act.activation(cat_hi[:, ds(h * T + CC * T, T)], hx[1][:], ACT.Copy).then_inc(cat_hi_ready, 1)

                split_hi(L, PC_ + 1, 0)
                load_table(ACT.Sqrt)
                for j in range(CC):
                    act.wait_ge(cent_ready, L * CC + (j + 1))
                    if j >= 2:
                        act.wait_ge(sq_added, L * NSQ + (Q_LN + j - 1))
                    act.activation(sq[j % 2][:], yc[:, ck(j)], ACT.Square).then_inc(sq_ready, 1)
                root(L, N_LN, 5, D_CONV)
                load_table(ACT.Silu)
                for j in range(CC):
                    act.wait_ge(norm_ready, L * CC + (j + 1))
                    act.activation(u[:, ck(j)], yc[:, ck(j)], ACT.Silu, scale=col(L, LN_G + j), bias=col(L, LN_B + j))
                    act.drain()
                    act.activation(cat_hi[:, ck(j)], u[:, ck(j)], ACT.Copy).then_inc(lnhi_ready, 1)

                for m in range(KC):
                    evacuate_m(L, L * NUNIT + (UC + m + 1), L * NSQ + (Q_MIX_POST + m), G_MIX_POST, m - m % 4, m % 4)
                    if m in (1, 3, 5):
                        split_hi(L, PC_ + 2 + m // 2, 0)

                load_table(ACT.Sqrt)
                root(L, N_MIX_POST, POST_BANK, DM)
                for c in range(KC):
                    act.wait_ge(x_new, L * (2 * KC) + (c + 1))
                    if c >= 2:
                        act.wait_ge(xsq_used, L * (KC - 1) + (c - 1))
                    act.activation(sq[c % 2][:], x[:, ck(c)], ACT.Square).then_inc(xsq_ready, 1)
                root(L, N_FFN_PRE, PRE_BANK, DM)
                split_h_hi(L, 1)

                with act.Fori(0, FC // 2) as i:
                    for s in range(2):
                        split_hi(L, PD + 1 + s, i)
                        for n in range(2):
                            dst = (tap_gate, tap_value)[n]
                            act.wait_ge(unit_ready, L * NUNIT + i * 4 + (UD + 2 * s + n + 1) + START)
                            act.wait_ge(a_ready, L * FC + i * 2 + s + START)
                            uc = 2 * s + n
                            act.activation(dst, bank[uc][:], ACT.Identity,
                                           scale=col(L, FW + uc * FTAPS + 2, i * (4 * FTAPS)),
                                           bias=col(L, FB + uc, i * 4)).then_inc(tap_ready, 1)
                        act.wait_ge(conv3_ready, L * (2 * FC) + i * 4 + (2 * s + 1))
                        act.activation(gelu, tap_gate, ACT.Gelu_apprx_tanh).then_inc(gelu_ready, 1)

                act.wait_ge(p_full, L * 16 + 16)
                act.wait_ge(unit_ready, L * NUNIT + UE + START)
                act.activation(h_hi[:, (KC - PC) * T:KC * T], praw, ACT.Copy).then_inc(p_hi_ready, 1)
                with act.Fori(0, 2) as i:
                    for q in range(4):
                        split_hi(L, PE_ + 1 + 2 * q, i * 4)
                        split_hi(L, PE_ + 2 + 2 * q, i * 4)
                        evacuate_m(L, L * NUNIT + i * 4 + (UE + q + 1), L * NSQ + i * 4 + (Q_FFN_POST + q),
                                   G_FFN_POST, i * 4, q)

                split_hi(L, PF + 1, 0)
                load_table(ACT.Sqrt)
                root(L, N_FFN_POST, POST_BANK, DM)
                for q in range(4):
                    act.wait_ge(unit_ready, L * NUNIT + (UF + q + 1) + START)
                    act.activation(pw[:, ck(q)], bank[q][:], ACT.Copy).then_inc(pw_ready, 1)
                split_hi(L, PF + 2, 0)

                def split_x_hi(c):
                    act.wait_ge(x_new, L * (2 * KC) + (KC + c + 1))
                    act.activation(h_hi[:, ck(c)], x[:, ck(c)], ACT.Copy).then_inc(x_hi_ready, 1)

                for q in range(4):
                    split_x_hi(q)
                    act.wait_ge(unit_ready, L * NUNIT + (UF + q + 5) + START)
                    act.activation(pw[:, ck(4 + q)], bank[q][:], ACT.Copy).then_inc(pw_ready, 1)
                for c in range(4, KC):
                    split_x_hi(c)
                load_table(ACT.Sigmoid)

                for m in range(KC):
                    if m % 2 == 0:
                        split_hi(L, PG + 1 + m // 2, 0)
                    act.wait_ge(unit_ready, L * NUNIT + (UG + m + 1) + START)
                    if m >= 2:
                        act.wait_ge(xg_new, L * KC + (m - 1) + START)
                    act.activation(gate[m % 2][:], bank[m % 4][:], ACT.Sigmoid).then_inc(gate_ready, 1)
                    if m >= 1:
                        act.wait_ge(xg_new, L * KC + m + START)
                        act.wait_ge(sq_added, L * NSQ + (Q_NEXT + m - 2))
                        act.activation(sq[(m - 1) % 2][:], x[:, ck(m - 1)], ACT.Square).then_inc(sq_ready, 1)

        @block.vector
        def _(dve):
            def split_lo(L, base, i, halves=(0, 1)):
                s = base % 2
                for half in halves:
                    c = slice(half * UNIT, (half + 1) * UNIT)
                    dve.wait_ge(hi_ready, L * (2 * NPAIR) + i * 4 + (2 * base + half + 1))
                    dve.tensor_tensor(w_lo[s][:, c], raw[s][:, c], w_hi[s][:, c].bitcast(F32), ALU.subtract).then_inc(lo_ready, 1)

            def add_square(n, L=0, dyn=0):
                dve.drain()
                dve.wait_ge(sq_ready, L * NSQ + dyn + (n + 1))
                dve.tensor_tensor(sumsq[:], sumsq[:], sq[n % 2][:], ALU.add).then_inc(sq_added, 1)

            def inverse(L, n, dyn=0):
                dve.wait_ge(root_done, L * NSTAT + dyn + (n + 1))
                dve.reciprocal(rstd_tok[:], std_tok[:]).then_inc(inverse_ready, 1)

            def wait_spread(L, n, dyn=0):
                dve.wait_ge(spread_done, L * NSTAT + dyn + (n + 1))

            def split_h_lo(L, phase, c):
                dve.wait_ge(hhi_ready, L * (2 * KC) + (phase * KC + c + 1))
                dve.tensor_tensor(h_lo[:, ck(c)], hx[c % 2][:], h_hi[:, ck(c)].bitcast(F32), ALU.subtract).then_inc(h_ready, 1)

            def make_h(L, phase, gain):
                for c in range(KC):
                    dve.scalar_tensor_tensor(out=hx[c % 2][:], in0=x[:, ck(c)], scalar=col(L, gain + c), in1=bank[PRE_BANK][:],
                                             op0=ALU.mult, op1=ALU.mult).then_inc(hx_ready, 1)
                    if c >= 1:
                        split_h_lo(L, phase, c - 1)
                    dve.drain()
                split_h_lo(L, phase, KC - 1)

            def tap(L, acc, j, d):
                w = col(L, CONV_W + TAPS - 1 - d, j * TAPS)
                src = u[:, ds(j * T, T - d)]
                out = yc[:, ds(j * T + d, T - d)] if acc is yc else acc[:, d:T]
                if d == 0:
                    return dve.tensor_scalar(out, src, w, col(L, CONV_B, j), ALU.mult, ALU.add)
                if d == 1:
                    return dve.tensor_scalar(out, src, w, None, ALU.mult)
                return dve.scalar_tensor_tensor(out=out, in0=src, scalar=w, in1=out, op0=ALU.mult, op1=ALU.add)

            def conv_steps(L, j, steps, end):
                for n in steps:
                    dve.drain()
                    tap(L, yc, j, 2 * n)
                    if 2 * n + 1 < TAPS:
                        tap(L, y_odd, j, 2 * n + 1)
                    if n == end - 1:
                        dve.drain()
                        dve.tensor_tensor(yc[:, ds(j * T, T)], yc[:, ds(j * T, T)], y_odd[:], ALU.add)

            def conv_rest(L, rounds):
                for d in rounds:
                    dve.drain()
                    for j in range(1, CC):
                        last = tap(L, yc, j, d)
                    if d == TAPS - 1:
                        last.then_inc(conv_done, 1)

            for signal in (u_ready, qk_read, probs_ready, o_read, rot_ready, gn_ready, cat_ready, a_ready, xg_new):
                dve.sem_inc(signal, START)
            dve.sem_inc(lo_ready, 4)
            dve.memset(sumsq[:], 0.0)
            for c in range(KC - 1):
                add_square(c)
            split_lo(0, 0, 0)
            dve.wait_ge(load_par, 16)

            with dve.Fori(0, DEPTH) as L:
                add_square(Q_MIX_PRE, L)
                inverse(L, N_MIX_PRE)
                dve.memset(sumsq[:], 0.0)
                dve.memset(y_odd[:, 0:1], 0.0)
                wait_spread(L, N_MIX_PRE)
                make_h(L, 0, G_MIX_PRE)

                for p in range(4):
                    split_lo(L, PA + p + 1, 0)
                    if p == 3:
                        dve.wait_ge(trig_ready, L * 2 + 2)
                        dve.wait_ge(load_mask, L * 16 + 16)
                    dve.wait_ge(sig_ready, L * CC + (p + 1))
                    dve.tensor_tensor(u[:, ck(p)], bank[2 * (p % 2)][:], sig[p % 2][:], ALU.mult).then_inc(u_ready, 1)
                    conv_steps(L, 0, range(5 * p, min(5 * p + 5, STEPS)), STEPS)

                def head(h, conv):
                    conv(0)
                    split_lo(L, PB + 1, h)
                    for n in range(2):
                        dve.drain()
                        dve.wait_ge(swap_ready, L * (2 * NH) + h * 2 + (n + 1))
                        dve.tensor_tensor(tqk[:], bank[n][:], cosT[:], ALU.mult).then_inc(qk_read, 1)
                        dve.tensor_tensor(swp[n][:], swp[n][:], sinT[:], ALU.mult)
                        dve.drain()
                        dve.wait_ge(scores_ready, L * (NH * NH) + h * NH + START)
                        dve.tensor_tensor(rot[n][:], tqk[:], swp[n][:], ALU.add).then_inc(rot_ready, 1)
                        conv(1 + n)
                    split_lo(L, PB + 2, h)
                    dve.wait_ge(o_done, L * NH + h + START)
                    for j in range(NH):
                        dve.wait_ge(scores_ready, L * (NH * NH) + h * NH + (j + 1) + START)
                        dve.tensor_tensor(probs[j][:], bank[S_BANK[j % 2]][:, 0:T - j * P],
                                          mask[:, ds(h * T, T - j * P)], ALU.mult).then_inc(probs_ready, 1)
                    conv(3)
                    inverse(L, N_HEAD, h)
                    conv(4)
                    dve.wait_ge(silu_ready, L * NH + h + 1 + START)
                    dve.scalar_tensor_tensor(out=hx[0][:], in0=bank[O_BANK][:], scalar=col(L, GN_G, h), in1=silu_g[:],
                                             op0=ALU.mult, op1=ALU.mult).then_inc(o_read, 1)
                    dve.drain()
                    wait_spread(L, N_HEAD, h)
                    dve.tensor_tensor(hx[1][:], bank[CV_BANK][:], hx[0][:], ALU.mult).then_inc(gn_ready, 1)
                    conv(5)
                    dve.wait_ge(cat_hi_ready, L * NH + h + 1)
                    dve.tensor_tensor(cat_lo[:, ds(h * T + CC * T, T)], hx[1][:],
                                      cat_hi[:, ds(h * T + CC * T, T)].bitcast(F32), ALU.subtract).then_inc(cat_ready, 1)

                slots = (0, 3, 5, 6, 10, 11, HEAD_STEPS)
                with dve.Fori(0, NH - 1) as h:
                    head(h, lambda n: conv_steps(L, h + 1, range(slots[n], slots[n + 1]), HEAD_STEPS))
                rest = range(2 * HEAD_STEPS, TAPS)
                rest_slots = (0, 2, 3, 4, len(rest), len(rest), len(rest))
                head(NH - 1, lambda n: conv_rest(L, rest[rest_slots[n]:rest_slots[n + 1]]))

                split_lo(L, PC_ + 1, 0)
                dve.wait_ge(mean_done, L + 1)
                for j in range(CC):
                    dve.scalar_tensor_tensor(out=yc[:, ck(j)], in0=bank[4][:], scalar=-1.0 / D_CONV, in1=yc[:, ck(j)],
                                             op0=ALU.mult, op1=ALU.add).then_inc(cent_ready, 1)
                    if j >= 1:
                        add_square(Q_LN + j - 1, L)
                add_square(Q_LN + CC - 1, L)
                inverse(L, N_LN)
                dve.memset(sumsq[:], 0.0)
                wait_spread(L, N_LN)
                for j in range(CC + 1):
                    if j < CC:
                        dve.tensor_tensor(yc[:, ck(j)], yc[:, ck(j)], bank[5][:], ALU.mult).then_inc(norm_ready, 1)
                    if j >= 1:
                        dve.wait_ge(lnhi_ready, L * CC + j)
                        dve.tensor_tensor(cat_lo[:, ck(j - 1)], u[:, ck(j - 1)], cat_hi[:, ck(j - 1)].bitcast(F32),
                                          ALU.subtract).then_inc(lncat_ready, 1)

                for m in range(KC):
                    add_square(Q_MIX_POST + m, L)
                    if m in (1, 3, 5):
                        split_lo(L, PC_ + 2 + m // 2, 0)

                def update_x(phase, n, split=lambda c: None):
                    inverse(L, n)
                    dve.memset(sumsq[:], 0.0)
                    wait_spread(L, n)
                    dve.wait_ge(m_ready, L * (2 * KC) + (phase + 1) * KC)
                    for c in range(KC + 2):
                        if c < KC:
                            dve.tensor_tensor(mT[:, ck(c)], mT[:, ck(c)], bank[POST_BANK][:], ALU.mult)
                        if 1 <= c < KC + 1:
                            dve.tensor_tensor(x[:, ck(c - 1)], x[:, ck(c - 1)], mT[:, ck(c - 1)], ALU.add).then_inc(x_new, 1)
                        dve.drain()
                        if c >= 2:
                            split(c - 2)
                        if c == 2 and phase == 1:
                            split_lo(L, PG, 0)

                update_x(0, N_MIX_POST)
                inverse(L, N_FFN_PRE)
                wait_spread(L, N_FFN_PRE)
                make_h(L, 1, G_FFN_PRE)

                with dve.Fori(0, FC // 2) as i:
                    for s in range(2):
                        split_lo(L, PD + 1 + s, i)
                        for n in range(2):
                            dst, uc = (tap_gate, tap_value)[n], 2 * s + n
                            dve.wait_ge(tap_ready, L * (2 * FC) + i * 4 + (uc + 1))
                            for back in (1, 2):
                                ins = dve.scalar_tensor_tensor(
                                    out=dst[:, back:T], in0=bank[uc][:, 0:T - back],
                                    scalar=col(L, FW + uc * FTAPS + 2 - back, i * (4 * FTAPS)),
                                    in1=dst[:, back:T], op0=ALU.mult, op1=ALU.add)
                                if back == 1:
                                    dve.drain()
                            ins.then_inc(conv3_ready, 1)
                        dve.drain()
                        dve.wait_ge(gelu_ready, L * FC + i * 2 + (s + 1))
                        dve.tensor_tensor(hidden, gelu, tap_value, ALU.mult)
                        dve.drain()
                        o = ds(i * (2 * T) + s * T, T)
                        dve.tensor_copy(a_hi[:, o], hidden)
                        dve.drain()
                        dve.tensor_tensor(a_lo[:, o], hidden, a_hi[:, o].bitcast(F32), ALU.subtract).then_inc(a_ready, 1)

                dve.wait_ge(p_hi_ready, L + 1)
                for k in range(PC):
                    c = KC - PC + k
                    dve.tensor_tensor(h_lo[:, ck(c)], praw[:, ck(k)], h_hi[:, ck(c)].bitcast(F32), ALU.subtract).then_inc(p_ready, 1)
                with dve.Fori(0, 2) as i:
                    for q in range(4):
                        split_lo(L, PE_ + 1 + 2 * q, i * 4)
                        split_lo(L, PE_ + 2 + 2 * q, i * 4)
                        add_square(Q_FFN_POST + q, L, i * 4)
                split_lo(L, PF + 1, 0)

                def x_lo(c):
                    dve.wait_ge(x_hi_ready, L * KC + (c + 1))
                    dve.tensor_tensor(h_lo[:, ck(c)], x[:, ck(c)], h_hi[:, ck(c)].bitcast(F32), ALU.subtract).then_inc(h_ready, 1)

                update_x(1, N_FFN_POST, x_lo)

                for m in range(KC):
                    if m % 2 == 0:
                        split_lo(L, PG + 1 + m // 2, 0)
                    dve.wait_ge(gate_ready, L * KC + (m + 1) + START)
                    dve.wait_ge(pw_ready, L * KC + KC)
                    dve.tensor_tensor(gate[m % 2][:], gate[m % 2][:], pw[:, ck(m)], ALU.mult)
                    dve.drain()
                    dve.tensor_tensor(x[:, ck(m)], x[:, ck(m)], gate[m % 2][:], ALU.add).then_inc(xg_new, 1)
                    if m >= 1:
                        add_square(Q_NEXT + m - 1, L)


def kernel(**inputs):
    import numpy as np
    import concourse.bacc as bacc
    from concourse.bass_utils import run_bass_kernel_spmd

    f32 = np.float32
    a = {k: np.asarray(v) for k, v in inputs.items()}

    def tiles(w, cols):
        c = w[:, cols:cols + P]
        return c.reshape(-1, P, P).transpose(1, 0, 2).reshape(P, -1)

    def unit_pairs(units):
        return [np.concatenate(units[n:n + 2], axis=1) for n in range(0, len(units), 2)]

    wa, wd, wp = [], [], []
    for L in range(DEPTH):
        w_in, w_out, up, down = a["w_in"][L], a["w_out"][L], a["ffn_up"][L], a["ffn_down"][L]
        units = []
        for j in range(CC):
            units += [tiles(w_in, j * P), tiles(w_in, D_CONV + j * P)]
        for h in range(NH):
            units += [tiles(w_in, 2 * D_CONV + g * NH * P + h * P) for g in range(4)]
        units += [tiles(w_out, m * P) for m in range(KC)]
        for j in range(FC):
            units += [tiles(up, D_FF + j * P), tiles(up, j * P)]
        units += [tiles(a["ple_gate"][L], m * P) for m in range(KC)]
        wa += unit_pairs(units)
        wd.append(np.stack([tiles(down, m * P)[:, s * HALF_DOWN:(s + 1) * HALF_DOWN] for m in range(KC) for s in range(2)]))
        ple = [tiles(a["ple_proj"][L], m * P) for m in range(KC)]
        wp.append(np.stack([np.concatenate(ple[4 * s:4 * s + 4], axis=1) for s in range(2)]))

    def cols(v):
        return np.ascontiguousarray(v.reshape(-1, P).T)

    params = []
    for L in range(DEPTH):
        cw = a["conv_w"][L].T.reshape(CC, P, TAPS).transpose(1, 0, 2).reshape(P, -1)
        fw = a["ffn_conv_w"][L].T.reshape(2, FC, P, FTAPS)[::-1].transpose(2, 1, 0, 3).reshape(P, -1)
        fb = a["ffn_conv_b"][L].reshape(2, FC, P)[::-1].transpose(2, 1, 0).reshape(P, -1)
        params += [cols(a[n][L]) for n in ("norm_mix_pre", "norm_mix_post", "norm_ffn_pre", "norm_ffn_post")]
        params += [cw, cols(a["conv_b"][L]), cols(a["conv_ln_g"][L]), cols(a["conv_ln_b"][L]), cols(a["ret_gn_g"][L]), fw, fb]
    params = np.concatenate(params, axis=1)

    n, m = np.arange(T)[None, :], np.arange(P)[:, None]
    masks = [np.where(n >= m, np.exp(np.log1p(-(2.0 ** (-5.0 - h))) * np.maximum(n - m, 0)), 0.0) * P ** -0.5 for h in range(NH)]
    inv_freq = f32(10000.0) ** (-(np.arange(P // 2, dtype=f32) / f32(P // 2)))
    consts = np.concatenate([np.eye(P) - 1.0 / P, np.eye(P), np.tile(inv_freq, 2)[:, None],
                                     np.repeat([-1.0, 1.0], P // 2)[:, None]], axis=1).astype(f32)

    arrays = {
        "xT": a["x"][0].T.reshape(KC, P, T),
        "pT": a["p"][:, 0].transpose(0, 2, 1).reshape(DEPTH, PC, P, T),
        "pos": a["positions"].reshape(1, T),
        "masks": np.concatenate(masks, axis=1).astype(f32), "consts": consts, "params": params,
        "wa": np.stack(wa + [np.zeros_like(wa[0])]), "wd": np.stack(wd), "wp": np.stack(wp),
    }
    arrays = {k: np.ascontiguousarray(v) for k, v in arrays.items()}
    nc = bacc.Bacc("TRN2", target_bir_lowering=False, num_devices=1, dynamic_dma_scratch_size=1024)
    aps = [nc.dram_tensor(k, v.shape, mybir.dt.from_np(v.dtype), kind="ExternalInput").ap() for k, v in arrays.items()]
    out = nc.dram_tensor("out", (KC, P, T), F32, kind="ExternalOutput").ap()
    build(nc, *aps, out)
    r = run_bass_kernel_spmd(nc, [arrays], core_ids=[0])
    y = r.results[0]["out"]
    return np.ascontiguousarray(y.reshape(DM, T).T)[None]
```

```python
from contextlib import ExitStack

import concourse.bass as bass
from concourse import mybir

ALU = mybir.AluOpType
ACT = mybir.ActivationFunctionType
F32 = mybir.dt.float32
F32R = mybir.dt.float32r
I32 = mybir.dt.int32
ds = bass.ds

P = 128
DEPTH = 2
T = 512
DM = 1024
KC = DM // P
D_CONV = 512
CC = D_CONV // P
TAPS = 31
NH = 4
D_FF = 2816
FC = D_FF // P
FTAPS = 3
PLE = 256
PC = PLE // P
EPS = 1e-6

TILE = P
UNIT = KC * TILE
PAIR = 2 * UNIT
HALF_DOWN = FC // 2 * TILE

PA, PB, PC_, PD, PE_, PF, PG, NPAIR = 0, 4, 12, 16, 38, 54, 56, 60
UA, UB, UC, UD, UE, UF, UG, NUNIT = 0, 8, 24, 32, 76, 84, 92, 100
WA_PAIRS = 42

G_MIX_PRE, G_MIX_POST, G_FFN_PRE, G_FFN_POST = 0, 8, 16, 24
CONV_W = 32
CONV_B = CONV_W + CC * TAPS
LN_G, LN_B, GN_G = CONV_B + 4, CONV_B + 8, CONV_B + 12
FW = CONV_B + 16
FB = FW + 2 * FC * FTAPS
NPAR = FB + 2 * FC

C_CENTER, C_IDENT = 0, P
C_INVF, C_SIGN = 2 * P, 2 * P + 1
NCONST = C_SIGN + 1

TWO_PI_A, TWO_PI_B, TWO_PI_C = 6.28125, 0.0019350051879882812, 3.0199e-07
ROUND_MAGIC = 12582912.0
BIG_TURNS = 2.0 ** 15

N_MIX_PRE, N_HEAD, N_LN, N_MIX_POST, N_FFN_PRE, N_FFN_POST, NSTAT = 0, 1, NH + 1, NH + 2, NH + 3, NH + 4, NH + 5
Q_LN, Q_MIX_POST, Q_FFN_POST, Q_NEXT = KC, KC + CC, 2 * KC + CC, 3 * KC + CC
NSQ = Q_NEXT

TB = T // P
STEPS = TAPS // 2 + 1
UP_BANKS = (6, 7)
MIX_BANKS = (0, 1, 2, 3, 6, 7, 0, 1)

CONV_BESIDE_A = (0, 0, 4, 6, 10, 12, 15, 16, 16)
CONV_BESIDE_HEAD = (0, 3, 4, 5, 10, 10, 11)
REST_BESIDE_HEAD = (22, 24, 24, 26, 29, 31, 31)
HEAD_STEPS = CONV_BESIDE_HEAD[-1]
UP_ORDER = [0, 0, 1, 0, 0, 0, 1, 1, 0, 1, 0, 0, 1, 1, 1, 1]
GATE_ORDER = [0, 0, 0, 1, 0, 0, 1, 0, 1, 0, 1, 0, 1, 1, 1, 1]
MLP_STAT_AT, MLP_SPREAD_AT = 1, 4
MEAN_AT, LN_SPREAD_AT = 4, 4
SPLIT_UP_AT, SPLIT_GATE_AT = 2, (0, 3)
HI_GATE_AT = 3
POST_SUM_AT, POST_SPREAD_AT = 2, 3

CHUNK_OPS = 2 * HEAD_STEPS + 1
REST_OPS = (CC - 1) * (TAPS - 2 * HEAD_STEPS)
CONV_OPS = (TAPS + 1) + (CC - 1) * CHUNK_OPS + REST_OPS

START = 1


def build(nc, xT, pT, pos, masks, consts, params, wa, wd, wp, out):
    with ExitStack() as ctx:
        def sb(name, shape, dt=F32, stack=ctx):
            return stack.enter_context(nc.sbuf_tensor(name, shape, dt))

        def sem(name):
            return ctx.enter_context(nc.semaphore(name))

        x = sb("x", [P, KC * T])
        h_hi, h_lo = sb("h_hi", [P, KC * T], F32R), sb("h_lo", [P, KC * T], F32R)
        mT = sb("mT", [P, KC * T])
        raw = [sb(f"raw{s}", [P, PAIR]) for s in range(2)]
        w_hi = [sb(f"w_hi{s}", [P, PAIR], F32R) for s in range(2)]
        w_lo = [sb(f"w_lo{s}", [P, PAIR], F32R) for s in range(2)]
        angle = sb("angle", [P, T])
        cosT, sinT = sb("cosT", [P, T]), sb("sinT", [P, T])
        cst = sb("cst", [P, NCONST])
        par = sb("par", [P, DEPTH * NPAR])
        ones = sb("ones", [P, P])
        eps = sb("eps", [P, 1])
        half_pi = sb("half_pi", [P, 1])
        sumsq = sb("sumsq", [P, T])
        sq = [sb(f"sq{s}", [P, T]) for s in range(2)]
        std_tok, rstd_tok = sb("std_tok", [P, TB]), sb("rstd_tok", [P, TB])
        junk = sb("junk", [P, 4])
        hx = [sb(f"hx{s}", [P, T]) for s in range(2)]
        positions = mT[:, 0:T].bitcast(I32)
        tap_gate, tap_value, gelu, hidden = (mT[:, n * T:(n + 1) * T] for n in range(4))
        z = [mT[:, n * T:(n + 1) * T] for n in (4, 5)]
        praw = mT[:, (KC - PC) * T:KC * T]

        with ExitStack() as mixer:
            cat_hi = sb("cat_hi", [P, KC * T], F32R, mixer)
            cat_lo = sb("cat_lo", [P, KC * T], F32R, mixer)
            u = sb("u", [P, CC * T], F32, mixer)
            yc = sb("yc", [P, CC * T], F32, mixer)
            y_odd = sb("y_odd", [P, T], F32, mixer)
            sig = [sb(f"sig{s}", [P, T], F32, mixer) for s in range(2)]
            swp = [sb(f"swp{s}", [P, T], F32, mixer) for s in range(2)]
            tqk = sb("tqk", [P, T], F32, mixer)
            rot = [sb(f"rot{s}", [P, T], F32, mixer) for s in range(2)]
            vT = sb("vT", [P, T], F32, mixer)
            vc = sb("vc", [P, T], F32, mixer)
            silu_g = sb("silu_g", [P, T], F32, mixer)
            probs = [sb(f"probs{j}", [P, T - j * P], F32, mixer) for j in range(NH)]
            osq = sb("osq", [P, T], F32, mixer)
            turns = sb("turns", [P, T], F32, mixer)
            mask = sb("mask", [P, NH * T], F32, mixer)
        with ExitStack() as mlp:
            a_hi = sb("a_hi", [P, FC * T], F32R, mlp)
            a_lo = sb("a_lo", [P, FC * T], F32R, mlp)
        with ExitStack() as embed:
            pw = sb("pw", [P, KC * T], F32, embed)
            gate = [sb(f"gate{s}", [P, T], F32, embed) for s in range(2)]
        sb("region", [P, 2 * FC * T])

        bank = [ctx.enter_context(nc.psum_tensor(f"bank{b}", [P, T], F32)) for b in range(8)]
        S_BANK, CV_BANK, O_BANK = (4, 5), 6, 7
        POST_BANK, PRE_BANK = 4, 5

        load_x = [sem(f"load_x{c}") for c in range(KC)]
        load_pos, load_cst, load_par = sem("load_pos"), sem("load_cst"), sem("load_par")
        load_mask, p_full, out_done = sem("load_mask"), sem("p_full"), sem("out_done")
        raw_full = [[sem(f"raw_full{s}{half}") for half in range(2)] for s in range(2)]
        ones_set, angle_ready = sem("ones_set"), sem("angle_ready")
        unit_ready, half_done, heads_mixed = sem("unit_ready"), sem("half_done"), sem("heads_mixed")
        scores_ready, vc_done, o_done, mean_done = sem("scores_ready"), sem("vc_done"), sem("o_done"), sem("mean_done")
        sums_done, spread_done = sem("sums_done"), sem("spread_done")
        hi_ready, hhi_ready, p_hi_ready, x_hi_ready = sem("hi_ready"), sem("hhi_ready"), sem("p_hi_ready"), sem("x_hi_ready")
        cat_hi_ready, lnhi_ready, a_hi_ready = sem("cat_hi_ready"), sem("lnhi_ready"), sem("a_hi_ready")
        root_done, sq_ready, xsq_ready, osq_ready = sem("root_done"), sem("sq_ready"), sem("xsq_ready"), sem("osq_ready")
        trig_ready, sig_ready, swap_ready = sem("trig_ready"), sem("sig_ready"), sem("swap_ready")
        vt_ready, vc_ready, silu_ready = sem("vt_ready"), sem("vc_ready"), sem("silu_ready")
        m_ready, tap_ready, gelu_ready = sem("m_ready"), sem("tap_ready"), sem("gelu_ready")
        pw_ready, gate_ready = sem("pw_ready"), sem("gate_ready")
        lo_ready, h_ready, p_ready = sem("lo_ready"), sem("h_ready"), sem("p_ready")
        cat_ready, lncat_ready, a_ready = sem("cat_ready"), sem("lncat_ready"), sem("a_ready")
        inverse_ready, sq_added, xsum_ready = sem("inverse_ready"), sem("sq_added"), sem("xsum_ready")
        hx_ready, u_ready, qk_read = sem("hx_ready"), sem("u_ready"), sem("qk_read")
        rot_ready, probs_ready = sem("rot_ready"), sem("probs_ready")
        o_read, gn_ready, conv_ops = sem("o_read"), sem("gn_ready"), sem("conv_ops")
        cent_ready, norm_ready = sem("cent_ready"), sem("norm_ready")
        x_steps, xg_new = sem("x_steps"), sem("xg_new")
        z_ready, tap_ops, hidden_ready = sem("z_ready"), sem("tap_ops"), sem("hidden_ready")

        block = ctx.enter_context(nc.Block())
        ck = lambda c: slice(c * T, (c + 1) * T)

        def col(L, c, dyn=0):
            return par[:, ds(L * NPAR + c + dyn, 1)]

        @block.sync
        def _(sp):
            wa_r = wa
            wd_r = wd.rearrange("l n p c -> (l n) p c")
            wp_r = wp.rearrange("l n p c -> (l n) p c")

            def load(L, base, i, s, src, row, width):
                for half in range(2):
                    c = slice(half * UNIT, min((half + 1) * UNIT, width))
                    sp.wait_ge(lo_ready, L * (2 * NPAIR) + i * 4 + (2 * (base + s) + half + 1))
                    sp.dma_start(raw[s][:, c], src[ds(row, 1), :, c].rearrange("a p c -> p (a c)")).then_inc(raw_full[s][half], 16)

            def load_a(L, n, i, s):
                load(L, n - s, i, s, wa_r, L * WA_PAIRS + i * 2 + n, PAIR)

            for c in range(KC):
                sp.dma_start(x[:, ck(c)], xT[c]).then_inc(load_x[c], 16)
            for half, small in ((0, (cst, consts, load_cst)), (1, (par, params, load_par))):
                c = slice(half * UNIT, (half + 1) * UNIT)
                sp.dma_start(raw[0][:, c], wa_r[0][:, c]).then_inc(raw_full[0][half], 16)
                dst, src, signal = small
                sp.dma_start(dst[:], src).then_inc(signal, 16)
            sp.dma_start(positions, pos.broadcast_to([P, T])).then_inc(load_pos, 16)
            with sp.Fori(0, DEPTH) as L:
                load_a(L, 1, 0, 1)
                load_a(L, 2, 0, 0)
                load_a(L, 3, 0, 1)
                sp.wait_ge(unit_ready, L * NUNIT + START)
                sp.dma_start(mask[:], masks).then_inc(load_mask, 16)
                with sp.Fori(0, (PE_ - PB) // 2) as i:
                    for s in range(2):
                        load_a(L, PB + s, i, s)
                sp.wait_ge(x_steps, L * (4 * KC) + 2 * KC)
                sp.dma_start(praw.rearrange("p (k t) -> p k t", k=PC),
                             pT[ds(L, 1), :, :, :].rearrange("a k p t -> p (a k) t")).then_inc(p_full, 16)
                with sp.Fori(0, KC) as i:
                    for s in range(2):
                        load(L, PE_, i, s, wd_r, (L * KC + i) * 2 + s, HALF_DOWN)
                for s in range(2):
                    load(L, PF, 0, s, wp_r, L * 2 + s, HALF_DOWN)
                with sp.Fori(0, 2) as i:
                    for s in range(2):
                        load(L, PG, i, s, wa_r, L * WA_PAIRS + i * 2 + (PE_ + s), PAIR)
                load(L, NPAIR, 0, 0, wa_r, L * WA_PAIRS + WA_PAIRS, PAIR)
            for c in range(KC):
                sp.wait_ge(xg_new, KC * (DEPTH - 1) + c + 1 + START)
                sp.dma_start(out[c], x[:, ck(c)]).then_inc(out_done, 16)
            sp.wait_ge(out_done, 16 * KC)

        @block.gpsimd
        def _(pool):
            pool.memset(ones[:], 1.0).then_inc(ones_set, 1)
            pool.memset(eps[:], EPS).then_inc(ones_set, 1)
            pool.memset(half_pi[:], 1.5707963267948966).then_inc(ones_set, 1)
            pool.wait_ge(load_pos, 16)
            pool.wait_ge(load_cst, 16)
            pool.tensor_copy(angle[:], positions)
            pool.drain()
            pool.tensor_scalar(angle[:], angle[:], cst[:, C_INVF:C_INVF + 1], None, ALU.mult)
            two_pi = 6.283185307179586
            for turn in (BIG_TURNS, 1.0):
                pool.drain()
                pool.tensor_scalar(turns[:], angle[:], 1.0 / (two_pi * turn), ROUND_MAGIC, ALU.mult, ALU.add)
                pool.drain()
                pool.tensor_scalar(turns[:], turns[:], -ROUND_MAGIC, None, ALU.add)
                for part in (TWO_PI_A, TWO_PI_B, TWO_PI_C):
                    pool.drain()
                    pool.tensor_scalar(tqk[:], turns[:], -part * turn, None, ALU.mult)
                    pool.drain()
                    pool.tensor_tensor(angle[:], angle[:], tqk[:], ALU.add)
            pool.drain()
            pool.tensor_scalar(angle[:], angle[:], 3.1415925, -3.1415925, ALU.min, ALU.max).then_inc(angle_ready, 1)

        @block.tensor
        def _(pe):
            def tri(dst, whi, wlo, rhi, rlo, first, last):
                pe.matmul(dst, whi, rhi, start=first, stop=False)
                pe.matmul(dst, whi, rlo, start=False, stop=False)
                return pe.matmul(dst, wlo, rhi, start=False, stop=last)

            def tile_of(s, t):
                return w_hi[s][:, t * TILE:(t + 1) * TILE], w_lo[s][:, t * TILE:(t + 1) * TILE]

            def weights(L, base, i, s, half):
                pe.wait_ge(lo_ready, L * (2 * NPAIR) + i * 4 + (4 + 2 * (base + s) + half + 1))

            def project_part(s, half, b, rhi, rlo, ks):
                for k in ks:
                    last = tri(bank[b][:], *tile_of(s, half * KC + k), rhi[:, ck(k)], rlo[:, ck(k)], k == 0, k == KC - 1)
                return last

            def project_unit(s, half, b, rhi, rlo):
                return project_part(s, half, b, rhi, rlo, range(KC)).then_inc(unit_ready, 1)

            def project_pair(s, b, k):
                for half in range(2):
                    last = project_part(s, half, b + half, h_hi, h_lo, (k,))
                    if k == KC - 1:
                        last.then_inc(unit_ready, 1)

            def two_pairs_as_inputs_come(L, base, banks, order, wait_input, before_second=lambda: None):
                done = [0, 0]
                for s in order:
                    k = done[s]
                    if k == 0:
                        if s == 1:
                            before_second()
                        weights(L, base, 0, s, 1)
                    if s == 0:
                        wait_input(k)
                    assert s == 0 or k < done[0]
                    project_pair(s, banks[s], k)
                    done[s] += 1

            def token_sums(b, src, first=True, last=True):
                for j in range(TB):
                    ins = pe.matmul(bank[b][:, j:j + 1], src[:, j * P:(j + 1) * P], ones[:, 0:1],
                                    start=first and j == 0, stop=last and j == TB - 1, skip_group_check=True)
                return ins

            def sums_of_squares(L, count, b):
                pe.wait_ge(sq_added, L * NSQ + count)
                token_sums(b, sumsq).then_inc(sums_done, 1)

            def spread(L, n, b, dyn=0):
                pe.wait_ge(inverse_ready, L * NSTAT + dyn + (n + 1))
                for j in range(TB):
                    ins = pe.matmul(bank[b][:, j * P:(j + 1) * P], rstd_tok[:, j:j + 1].broadcast_to([P, P]),
                                    cst[:, C_IDENT:C_IDENT + P], start=(j == 0), stop=(j == TB - 1), skip_group_check=True)
                ins.then_inc(spread_done, 1)

            for signal in (unit_ready, scores_ready, vc_done, o_done):
                pe.sem_inc(signal, START)
            pe.wait_ge(ones_set, 3)
            pe.wait_ge(load_cst, 16)
            with pe.Fori(0, DEPTH) as L:
                sums_of_squares(L, Q_LN, PRE_BANK)
                spread(L, N_MIX_PRE, PRE_BANK)

                for p in range(4):
                    s = p % 2
                    weights(L, PA, 0, 0, 2 * p)
                    weights(L, PA, 0, 0, 2 * p + 1)
                    if p == 0:
                        pe.wait_ge(gate_ready, L * KC + START)
                        for k in range(KC):
                            pe.wait_ge(h_ready, L * (3 * KC) + (k + 1))
                            project_pair(s, 0, k)
                    else:
                        if p >= 2:
                            pe.wait_ge(u_ready, L * CC + (p - 1) + START)
                        project_unit(s, 0, 2 * s, h_hi, h_lo)
                        if p >= 2:
                            pe.wait_ge(sig_ready, L * CC + (p - 1))
                        project_unit(s, 1, 2 * s + 1, h_hi, h_lo)

                with pe.Fori(0, NH) as h:
                    weights(L, PB, h, 0, 0)
                    pe.wait_ge(u_ready, L * CC + CC - 1 + START)
                    pe.wait_ge(qk_read, L * (2 * NH) + h * 2 + START)
                    project_unit(0, 0, 0, h_hi, h_lo)
                    weights(L, PB, h, 0, 1)
                    project_unit(0, 1, 1, h_hi, h_lo)
                    weights(L, PB, h, 1, 0)
                    pe.wait_ge(u_ready, L * CC + CC + START)
                    pe.wait_ge(vt_ready, L * NH + h + START)
                    project_unit(1, 0, 2, h_hi, h_lo)
                    pe.wait_ge(rot_ready, L * (2 * NH) + h * 2 + 2 + START)
                    for j in range(NH):
                        pe.wait_ge(probs_ready, L * (NH * NH) + h * NH + max(j - 1, 0) + START)
                        pe.matmul(bank[S_BANK[j % 2]][:, 0:T - j * P], rot[1][:, j * P:(j + 1) * P], rot[0][:, j * P:T],
                                  start=True, stop=True).then_inc(scores_ready, 1)
                    pe.wait_ge(vt_ready, L * NH + h + 1 + START)
                    pe.wait_ge(gn_ready, L * NH + h + START)
                    for j in range(NH):
                        last = pe.matmul(bank[CV_BANK][:, j * P:(j + 1) * P], vT[:, j * P:(j + 1) * P],
                                         cst[:, C_CENTER:C_CENTER + P], start=(j == 0), stop=(j == NH - 1),
                                         skip_group_check=True)
                    last.then_inc(vc_done, 1)
                    weights(L, PB, h, 1, 1)
                    pe.wait_ge(silu_ready, L * NH + h + START)
                    project_part(1, 1, 3, h_hi, h_lo, range(0, 3))
                    pe.wait_ge(vc_ready, L * NH + h + 1)
                    pe.wait_ge(o_read, L * NH + h + START)
                    for j in range(NH):
                        pe.wait_ge(probs_ready, L * (NH * NH) + h * NH + (j + 1) + START)
                        last = pe.matmul(bank[O_BANK][:, j * P:T], vc[:, j * P:(j + 1) * P], probs[j][:],
                                         start=(j == 0), stop=(j == NH - 1), skip_group_check=True)
                    last.then_inc(o_done, 1)
                    project_part(1, 1, 3, h_hi, h_lo, range(3, 5))
                    pe.wait_ge(osq_ready, L * NH + h + 1)
                    token_sums(CV_BANK, osq).then_inc(sums_done, 1)
                    project_part(1, 1, 3, h_hi, h_lo, range(5, KC)).then_inc(unit_ready, 1)
                    spread(L, N_HEAD, CV_BANK, h)

                def mix_part(s, slot, m, k):
                    return tri(bank[MIX_BANKS[m]][:], *tile_of(s, slot * CC + k % CC), cat_hi[:, ck(k)], cat_lo[:, ck(k)],
                               k == CC, k == CC - 1)

                weights(L, PC_, 0, 0, 1)
                pe.wait_ge(silu_ready, L * NH + NH + START)
                for k in range(CC, KC):
                    pe.wait_ge(cat_ready, L * NH + (k - CC + 1) + START)
                    for m in range(4):
                        last = mix_part(0, m, m, k)
                    if k == KC - 1:
                        last.then_inc(heads_mixed, 1)
                    if k == MEAN_AT:
                        pe.wait_ge(conv_ops, L * CONV_OPS + CONV_OPS)
                        for j in range(CC):
                            last = pe.matmul(bank[4][:], ones[:], yc[:, ck(j)], start=(j == 0), stop=(j == CC - 1))
                        last.then_inc(mean_done, 1)
                sums_of_squares(L, Q_MIX_POST, 5)
                weights(L, PC_, 0, 0, 3)
                for k in range(CC, KC):
                    for m in (4, 5):
                        mix_part(1, m - 4, m, k)
                    if k == LN_SPREAD_AT:
                        spread(L, N_LN, 5)
                for k in range(CC):
                    pe.wait_ge(lncat_ready, L * CC + (k + 1))
                    for m in (0, 1):
                        last = mix_part(1, m + 2, m, k)
                        if k == CC - 1:
                            last.then_inc(unit_ready, 1)
                weights(L, PC_ + 2, 0, 0, 1)
                for m in range(2, 6):
                    for k in range(CC):
                        last = mix_part(0, m - 2, m, k)
                    last.then_inc(unit_ready, 1)
                weights(L, PC_ + 2, 0, 1, 1)
                for m in (6, 7):
                    pe.wait_ge(m_ready, L * (2 * KC) + (m - 5))
                    project_unit(1, m - 6, MIX_BANKS[m], cat_hi, cat_lo)
                sums_of_squares(L, Q_FFN_POST, POST_BANK)
                spread(L, N_MIX_POST, POST_BANK)

                def up_pair(i, s):
                    weights(L, PD, i, s, 1)
                    for half in range(2):
                        pe.wait_ge(z_ready, L * (2 * FC) + i * 4 + (2 * s + half - 3))
                        project_unit(s, half, 2 * s + half, h_hi, h_lo)

                two_pairs_as_inputs_come(L, PD, (UP_BANKS[0], 2), UP_ORDER, lambda k: pe.wait_ge(h_ready, L * (3 * KC) + (KC + k + 1)))
                weights(L, PD + 2, 0, 0, 1)
                for half in range(2):
                    ks = range(KC)
                    if half == 0:
                        project_part(0, 0, 0, h_hi, h_lo, ks[:MLP_STAT_AT])
                        pe.wait_ge(xsum_ready, L + 1)
                        token_sums(PRE_BANK, mT).then_inc(sums_done, 1)
                        project_part(0, 0, 0, h_hi, h_lo, ks[MLP_STAT_AT:MLP_SPREAD_AT])
                        spread(L, N_FFN_PRE, PRE_BANK)
                        ks = ks[MLP_SPREAD_AT:]
                    project_part(0, half, half, h_hi, h_lo, ks).then_inc(unit_ready, 1)
                with pe.Fori(1, FC // 2 - 1) as i:
                    for s in (1, 2):
                        up_pair(i + s // 2, s % 2)
                up_pair(FC // 2 - 1, 1)

                with pe.Fori(0, 2) as i:
                    for q in range(4):
                        if q in (0, 2):
                            pe.wait_ge(z_ready, L * (2 * FC) + (2 * FC - 2 + q))
                        pe.wait_ge(m_ready, L * (2 * KC) + i * 4 + (KC + q - 3 if q else KC - 3))
                        for s in range(2):
                            pe.wait_ge(lo_ready, L * (2 * NPAIR) + i * 16 + (4 + 2 * (PE_ + 2 * q + s) + 2))
                            pe.wait_ge(a_ready, L * FC + (FC // 2, FC - 1)[s] + START)
                            for t in range(FC // 2):
                                if s == 1 and t == FC // 2 - 1:
                                    pe.wait_ge(a_ready, L * FC + FC + START)
                                k = s * (FC // 2) + t
                                last = tri(bank[q][:], *tile_of(s, t), a_hi[:, ck(k)], a_lo[:, ck(k)], k == 0, k == FC - 1)
                            last.then_inc((half_done, unit_ready)[s], 1)

                for s in range(2):
                    weights(L, PF, 0, s, 1)
                    if s == 0:
                        pe.wait_ge(p_ready, L * PC + PC)
                    for q in range(4):
                        if s == 0:
                            pe.wait_ge(m_ready, L * (2 * KC) + (KC + 5 + q))
                        else:
                            pe.wait_ge(pw_ready, L * KC + (q + 1))
                        for k in range(PC):
                            c = KC - PC + k
                            last = tri(bank[q][:], *tile_of(s, q * PC + k), h_hi[:, ck(c)], h_lo[:, ck(c)], k == 0, k == PC - 1)
                        last.then_inc(unit_ready, 1)
                        if s * 4 + q == POST_SUM_AT:
                            sums_of_squares(L, Q_NEXT, POST_BANK)
                        if s * 4 + q == POST_SPREAD_AT:
                            spread(L, N_FFN_POST, POST_BANK)

                pe.wait_ge(pw_ready, L * KC + KC - 2)
                two_pairs_as_inputs_come(L, PG, (0, 2), GATE_ORDER, lambda k: pe.wait_ge(h_ready, L * (3 * KC) + (2 * KC + k + 1)),
                                         lambda: pe.wait_ge(pw_ready, L * KC + KC))
                for s in range(2):
                    for half in range(2):
                        weights(L, PG + 2, 0, s, half)
                        pe.wait_ge(gate_ready, L * KC + (2 * s + half + 1) + START)
                        project_unit(s, half, 2 * s + half, h_hi, h_lo)

        @block.scalar
        def _(act):
            def split_hi(L, base, i, width=PAIR):
                s = base % 2
                last = base - 2
                if last == PC_:
                    act.wait_ge(heads_mixed, L + 1)
                elif last == PC_ + 2:
                    act.wait_ge(unit_ready, L * NUNIT + (UC + 6) + START)
                elif last == PC_ + 1:
                    act.wait_ge(unit_ready, L * NUNIT + (UC + 2) + START)
                elif last < PE_:
                    act.wait_ge(unit_ready, L * NUNIT + i * 4 + max(2 * last + 2, 0) + START)
                elif last >= PG:
                    act.wait_ge(unit_ready, L * NUNIT + (UG + 2 * (last - PG + 1)) + START)
                elif last >= PF:
                    act.wait_ge(unit_ready, L * NUNIT + (UF + 4 * (last - PF + 1)) + START)
                elif (last - PE_) % 2 == 0:
                    act.wait_ge(half_done, L * KC + i + ((last - PE_) // 2 + 1))
                else:
                    act.wait_ge(unit_ready, L * NUNIT + i + (UE + (last - PE_ + 1) // 2) + START)
                for half in range(2):
                    c = slice(half * UNIT, min((half + 1) * UNIT, width))
                    act.wait_ge(raw_full[s][half], L * (16 * NPAIR // 2) + i * 16 + (16 * (base // 2 + 1)))
                    act.activation(w_hi[s][:, c], raw[s][:, c], ACT.Copy).then_inc(hi_ready, 1)

            def load_table(func):
                act.activation(junk[:, 0:1], eps[:, 0:1], func)
                act.drain()

            def root(L, n, b, features, dyn=0):
                act.wait_ge(sums_done, L * NSTAT + dyn + (n + 1))
                act.activation(std_tok[:], bank[b][:, 0:TB], ACT.Sqrt, scale=1.0 / features, bias=eps[:, 0:1]).then_inc(root_done, 1)

            def split_h_hi(L):
                for c in range(KC):
                    act.wait_ge(hx_ready, L * KC + (c + 1))
                    act.activation(h_hi[:, ck(c)], hx[c % 2][:], ACT.Copy).then_inc(hhi_ready, 1)

            def evacuate_m(L, n_unit, n_sq, gain, dyn, m, b):
                act.wait_ge(unit_ready, n_unit + START)
                act.wait_ge(sq_added, n_sq - 1)
                act.activation(sq[m % 2][:], bank[b][:], ACT.Square).then_inc(sq_ready, 1)
                act.activation(mT[:, ds(dyn * T + m * T, T)], bank[b][:], ACT.Copy, scale=col(L, gain + m, dyn)).then_inc(m_ready, 1)

            for signal in (gate_ready, vt_ready, silu_ready):
                act.sem_inc(signal, START)
            act.wait_ge(ones_set, 3)
            load_table(ACT.Sqrt)
            for c in range(KC):
                act.wait_ge(load_x[c], 16)
                if c >= 2:
                    act.wait_ge(sq_added, c - 1)
                act.activation(sq[c % 2][:], x[:, ck(c)], ACT.Square).then_inc(sq_ready, 1)
            split_hi(0, 0, 0)
            act.wait_ge(load_par, 16)
            act.wait_ge(load_cst, 16)

            with act.Fori(0, DEPTH) as L:
                load_table(ACT.Sqrt)
                root(L, N_MIX_PRE, PRE_BANK, DM)
                split_h_hi(L)

                for p in range(4):
                    split_hi(L, PA + p + 1, 0)
                    if p == 2:
                        act.wait_ge(angle_ready, 1)
                        act.activation(cosT[:], angle[:], ACT.Abs)
                        act.activation(sinT[:], angle[:], ACT.Sin, scale=cst[:, C_SIGN:C_SIGN + 1]).then_inc(trig_ready, 1)
                        act.drain()
                        act.activation(cosT[:], cosT[:], ACT.Sin, scale=-1.0, bias=half_pi[:, 0:1]).then_inc(trig_ready, 1)
                    load_table(ACT.Sigmoid)
                    act.wait_ge(unit_ready, L * NUNIT + (UA + 2 * p + 2) + START)
                    if p >= 2:
                        act.wait_ge(u_ready, L * CC + (p - 1) + START)
                    act.activation(sig[p % 2][:], bank[2 * (p % 2) + 1][:], ACT.Sigmoid).then_inc(sig_ready, 1)

                with act.Fori(0, NH) as h:
                    split_hi(L, PB + 1, h)
                    for n in range(2):
                        act.wait_ge(unit_ready, L * NUNIT + h * 4 + (UB + n + 1) + START)
                        act.wait_ge(rot_ready, L * (2 * NH) + h * 2 + START)
                        act.activation(swp[n][0:64, :], bank[n][64:128, :], ACT.Copy)
                        act.activation(swp[n][64:128, :], bank[n][0:64, :], ACT.Copy).then_inc(swap_ready, 1)
                    split_hi(L, PB + 2, h)
                    act.wait_ge(unit_ready, L * NUNIT + h * 4 + (UB + 3) + START)
                    act.wait_ge(vc_done, L * NH + h + START)
                    act.activation(vT[:], bank[2][:], ACT.Copy).then_inc(vt_ready, 1)
                    act.wait_ge(vc_done, L * NH + h + 1 + START)
                    act.wait_ge(o_done, L * NH + h + START)
                    act.activation(vc[:], bank[CV_BANK][:], ACT.Copy).then_inc(vc_ready, 1)
                    load_table(ACT.Sqrt)
                    act.wait_ge(o_done, L * NH + h + 1 + START)
                    act.activation(osq[:], bank[O_BANK][:], ACT.Square).then_inc(osq_ready, 1)
                    root(L, N_HEAD, CV_BANK, P, h)
                    load_table(ACT.Silu)
                    act.wait_ge(unit_ready, L * NUNIT + h * 4 + (UB + 4) + START)
                    act.wait_ge(o_read, L * NH + h + START)
                    act.activation(silu_g[:], bank[3][:], ACT.Silu).then_inc(silu_ready, 1)
                    act.wait_ge(gn_ready, L * NH + h + 1 + START)
                    act.activation(cat_hi[:, ds(h * T + CC * T, T)], hx[1][:], ACT.Copy).then_inc(cat_hi_ready, 1)

                split_hi(L, PC_ + 1, 0)
                load_table(ACT.Sqrt)
                for j in range(CC):
                    act.wait_ge(cent_ready, L * CC + (j + 1))
                    if j >= 2:
                        act.wait_ge(sq_added, L * NSQ + (Q_LN + j - 1))
                    act.activation(sq[j % 2][:], yc[:, ck(j)], ACT.Square).then_inc(sq_ready, 1)
                root(L, N_LN, 5, D_CONV)
                split_hi(L, PC_ + 2, 0)
                load_table(ACT.Silu)
                for j in range(CC):
                    act.wait_ge(norm_ready, L * CC + (j + 1))
                    act.activation(u[:, ck(j)], yc[:, ck(j)], ACT.Silu, scale=col(L, LN_G + j), bias=col(L, LN_B + j))
                    act.drain()
                    act.activation(cat_hi[:, ck(j)], u[:, ck(j)], ACT.Copy).then_inc(lnhi_ready, 1)

                for m in range(KC):
                    evacuate_m(L, L * NUNIT + (UC + m + 1), L * NSQ + (Q_MIX_POST + m), G_MIX_POST, 0, m, MIX_BANKS[m])
                    if m in (1, 5):
                        split_hi(L, PC_ + 3 + m // 5, 0)

                load_table(ACT.Sqrt)
                root(L, N_MIX_POST, POST_BANK, DM)
                split_hi(L, PD + 1, 0)
                for c in range(KC):
                    act.wait_ge(x_steps, L * (4 * KC) + 2 * (c + 1))
                    act.activation(h_hi[:, ck(c)], x[:, ck(c)], ACT.Copy, scale=col(L, G_FFN_PRE + c)).then_inc(hhi_ready, 1)
                    act.activation(mT[:, ck(c)], x[:, ck(c)], ACT.Square).then_inc(xsq_ready, 1)
                split_hi(L, PD + 2, 0)
                root(L, N_FFN_PRE, PRE_BANK, DM)
                split_hi(L, PD + 3, 0)

                def mlp_chunk(i, s, split=True):
                    if split:
                        split_hi(L, PD + 2 + s, i)
                    for n in range(2):
                        uc = 2 * s + n
                        act.wait_ge(z_ready, L * (2 * FC) + i * 4 + (uc + 1))
                        act.wait_ge(a_ready, L * FC + i * 2 + s + START)
                        act.activation((tap_gate, tap_value)[n], z[n], ACT.Identity,
                                       scale=col(L, FW + uc * FTAPS + 2, i * (4 * FTAPS)),
                                       bias=col(L, FB + uc, i * 4)).then_inc(tap_ready, 1)
                    act.wait_ge(tap_ops, L * (4 * FC) + i * 8 + (4 * s + 3))
                    act.activation(gelu, tap_gate, ACT.Gelu_apprx_tanh).then_inc(gelu_ready, 1)
                    act.wait_ge(hidden_ready, L * FC + i * 2 + (s + 1))
                    act.activation(a_hi[:, ds(i * (2 * T) + s * T, T)], hidden, ACT.Copy).then_inc(a_hi_ready, 1)

                mlp_chunk(0, 0, split=False)
                mlp_chunk(0, 1, split=False)
                with act.Fori(1, FC // 2) as i:
                    for s in range(2):
                        mlp_chunk(i, s)

                act.wait_ge(p_full, L * 16 + 16)
                act.wait_ge(unit_ready, L * NUNIT + UE + START)
                act.activation(h_hi[:, (KC - PC) * T:KC * T], praw, ACT.Copy).then_inc(p_hi_ready, 1)
                with act.Fori(0, 2) as i:
                    for q in range(4):
                        split_hi(L, PE_ + 2 + 2 * q, i * 4, HALF_DOWN)
                        split_hi(L, PE_ + 3 + 2 * q, i * 4, HALF_DOWN)
                        evacuate_m(L, L * NUNIT + i * 4 + (UE + q + 1), L * NSQ + i * 4 + (Q_FFN_POST + q),
                                   G_FFN_POST, i * 4, q, q)

                load_table(ACT.Sqrt)
                root(L, N_FFN_POST, POST_BANK, DM)
                for q in range(4):
                    act.wait_ge(unit_ready, L * NUNIT + (UF + q + 1) + START)
                    act.activation(pw[:, ck(q)], bank[q][:], ACT.Copy).then_inc(pw_ready, 1)
                split_hi(L, PF + 2, 0)

                def split_x_hi(c):
                    act.wait_ge(x_steps, L * (4 * KC) + 2 * (KC + c + 1))
                    act.activation(h_hi[:, ck(c)], x[:, ck(c)], ACT.Copy).then_inc(x_hi_ready, 1)

                def take_pw(q):
                    act.wait_ge(unit_ready, L * NUNIT + (UF + q + 5) + START)
                    act.activation(pw[:, ck(4 + q)], bank[q][:], ACT.Copy).then_inc(pw_ready, 1)

                split_x_hi(0)
                take_pw(0)
                split_x_hi(1)
                for q in (1, 2, 3):
                    take_pw(q)
                for c in range(2, KC):
                    if c == HI_GATE_AT:
                        split_hi(L, PG + 1, 0)
                    split_x_hi(c)
                load_table(ACT.Sigmoid)

                def square_x(m):
                    act.wait_ge(xg_new, L * KC + m + 1 + START)
                    act.wait_ge(sq_added, L * NSQ + (Q_NEXT + m - 1))
                    act.activation(sq[m % 2][:], x[:, ck(m)], ACT.Square).then_inc(sq_ready, 1)

                for m in range(KC):
                    if m in (2, 4, 6):
                        split_hi(L, PG + 1 + m // 2, 0)
                    if m >= 1:
                        square_x(m - 1)
                    act.wait_ge(unit_ready, L * NUNIT + (UG + m + 1) + START)
                    act.activation(gate[m % 2][:], bank[m % 4][:], ACT.Sigmoid).then_inc(gate_ready, 1)
                load_table(ACT.Sqrt)
                square_x(KC - 1)

        @block.vector
        def _(dve):
            def split_lo(L, base, i, width=PAIR):
                s = base % 2
                for half in range(2):
                    c = slice(half * UNIT, min((half + 1) * UNIT, width))
                    dve.wait_ge(hi_ready, L * (2 * NPAIR) + i * 4 + (2 * base + half + 1))
                    dve.tensor_tensor(w_lo[s][:, c], raw[s][:, c], w_hi[s][:, c].bitcast(F32), ALU.subtract).then_inc(lo_ready, 1)

            def add_square(n, L=0, dyn=0):
                dve.drain()
                dve.wait_ge(sq_ready, L * NSQ + dyn + (n + 1))
                dve.tensor_tensor(sumsq[:], sumsq[:], sq[n % 2][:], ALU.add).then_inc(sq_added, 1)

            def inverse(L, n, dyn=0):
                dve.wait_ge(root_done, L * NSTAT + dyn + (n + 1))
                dve.reciprocal(rstd_tok[:], std_tok[:]).then_inc(inverse_ready, 1)

            def wait_spread(L, n, dyn=0):
                dve.wait_ge(spread_done, L * NSTAT + dyn + (n + 1))

            def split_h_lo(L, c):
                dve.wait_ge(hhi_ready, L * (2 * KC) + (c + 1))
                dve.tensor_tensor(h_lo[:, ck(c)], hx[c % 2][:], h_hi[:, ck(c)].bitcast(F32), ALU.subtract).then_inc(h_ready, 1)

            def make_h(L):
                for c in range(KC):
                    if c >= 2:
                        dve.wait_ge(h_ready, L * (3 * KC) + (c - 1))
                    dve.scalar_tensor_tensor(out=hx[c % 2][:], in0=x[:, ck(c)], scalar=col(L, G_MIX_PRE + c), in1=bank[PRE_BANK][:],
                                             op0=ALU.mult, op1=ALU.mult).then_inc(hx_ready, 1)
                    if c >= 1:
                        split_h_lo(L, c - 1)
                split_h_lo(L, KC - 1)

            def tap(L, acc, j, d):
                w = col(L, CONV_W + TAPS - 1 - d, j * TAPS)
                src = u[:, ds(j * T, T - d)]
                out = yc[:, ds(j * T + d, T - d)] if acc is yc else acc[:, d:T]
                if d == 0:
                    ins = dve.tensor_scalar(out, src, w, col(L, CONV_B, j), ALU.mult, ALU.add)
                elif d == 1:
                    ins = dve.tensor_scalar(out, src, w, None, ALU.mult)
                else:
                    ins = dve.scalar_tensor_tensor(out=out, in0=src, scalar=w, in1=out, op0=ALU.mult, op1=ALU.add)
                return ins.then_inc(conv_ops, 1)

            def conv_steps(L, j, steps, end, done):
                base = L * CONV_OPS + (0 if done is None else done)
                for n in steps:
                    for d in (2 * n, 2 * n + 1):
                        if d < TAPS:
                            if d >= 2 or (d == 1 and done is not None):
                                dve.wait_ge(conv_ops, base + (d - 1))
                            tap(L, (yc, y_odd)[d % 2], j, d)
                    if n == end - 1:
                        ops = min(2 * end, TAPS)
                        dve.wait_ge(conv_ops, base + ops)
                        dve.tensor_tensor(yc[:, ds(j * T, T)], yc[:, ds(j * T, T)], y_odd[:], ALU.add).then_inc(conv_ops, 1)

            def conv_rest(L, rounds):
                for d in rounds:
                    for j in range(1, CC):
                        n = (d - 2 * HEAD_STEPS) * (CC - 1) + j
                        dve.wait_ge(conv_ops, L * CONV_OPS + (CONV_OPS - REST_OPS + n - (CC - 1)))
                        tap(L, yc, j, d)

            for signal in (u_ready, qk_read, probs_ready, o_read, rot_ready, gn_ready, cat_ready, a_ready, xg_new):
                dve.sem_inc(signal, START)
            dve.sem_inc(lo_ready, 4)
            dve.memset(sumsq[:], 0.0)
            for c in range(KC):
                add_square(c)
            split_lo(0, 0, 0)
            dve.wait_ge(load_par, 16)

            with dve.Fori(0, DEPTH) as L:
                inverse(L, N_MIX_PRE)
                dve.memset(sumsq[:], 0.0)
                dve.memset(y_odd[:, 0:1], 0.0)
                wait_spread(L, N_MIX_PRE)
                make_h(L)

                for p in range(4):
                    conv_steps(L, 0, range(CONV_BESIDE_A[2 * p], CONV_BESIDE_A[2 * p + 1]), STEPS, None)
                    split_lo(L, PA + p + 1, 0)
                    if p == 3:
                        dve.wait_ge(trig_ready, L * 2 + 2)
                        dve.wait_ge(load_mask, L * 16 + 16)
                    dve.wait_ge(sig_ready, L * CC + (p + 1))
                    dve.tensor_tensor(u[:, ck(p)], bank[2 * (p % 2)][:], sig[p % 2][:], ALU.mult).then_inc(u_ready, 1)
                    if p == 0:
                        dve.wait_ge(u_ready, L * CC + 1 + START)
                    conv_steps(L, 0, range(CONV_BESIDE_A[2 * p + 1], CONV_BESIDE_A[2 * p + 2]), STEPS, None)

                def head(h, conv):
                    conv(0)
                    split_lo(L, PB + 1, h)
                    for n in range(2):
                        dve.drain()
                        dve.wait_ge(swap_ready, L * (2 * NH) + h * 2 + (n + 1))
                        dve.tensor_tensor(tqk[:], bank[n][:], cosT[:], ALU.mult).then_inc(qk_read, 1)
                        dve.tensor_tensor(swp[n][:], swp[n][:], sinT[:], ALU.mult)
                        dve.drain()
                        dve.wait_ge(scores_ready, L * (NH * NH) + h * NH + START)
                        dve.tensor_tensor(rot[n][:], tqk[:], swp[n][:], ALU.add).then_inc(rot_ready, 1)
                        conv(1 + n)
                    dve.wait_ge(o_done, L * NH + h + START)
                    for j in range(NH):
                        dve.wait_ge(scores_ready, L * (NH * NH) + h * NH + (j + 1) + START)
                        dve.tensor_tensor(probs[j][:], bank[S_BANK[j % 2]][:, 0:T - j * P],
                                          mask[:, ds(h * T, T - j * P)], ALU.mult).then_inc(probs_ready, 1)
                    split_lo(L, PB + 2, h)
                    conv(3)
                    inverse(L, N_HEAD, h)
                    conv(4)
                    dve.wait_ge(silu_ready, L * NH + h + 1 + START)
                    dve.scalar_tensor_tensor(out=hx[0][:], in0=bank[O_BANK][:], scalar=col(L, GN_G, h), in1=silu_g[:],
                                             op0=ALU.mult, op1=ALU.mult).then_inc(o_read, 1)
                    dve.drain()
                    wait_spread(L, N_HEAD, h)
                    dve.tensor_tensor(hx[1][:], bank[CV_BANK][:], hx[0][:], ALU.mult).then_inc(gn_ready, 1)
                    conv(5)
                    dve.wait_ge(cat_hi_ready, L * NH + h + 1)
                    dve.tensor_tensor(cat_lo[:, ds(h * T + CC * T, T)], hx[1][:],
                                      cat_hi[:, ds(h * T + CC * T, T)].bitcast(F32), ALU.subtract).then_inc(cat_ready, 1)

                with dve.Fori(0, NH - 1) as h:
                    head(h, lambda n: conv_steps(L, h + 1, range(CONV_BESIDE_HEAD[n], CONV_BESIDE_HEAD[n + 1]), HEAD_STEPS,
                                                 h * CHUNK_OPS + (TAPS + 1)))
                head(NH - 1, lambda n: conv_rest(L, range(REST_BESIDE_HEAD[n], REST_BESIDE_HEAD[n + 1])))

                conv_rest(L, range(REST_BESIDE_HEAD[6], TAPS))
                split_lo(L, PC_ + 1, 0)
                dve.wait_ge(mean_done, L + 1)
                for j in range(CC):
                    dve.scalar_tensor_tensor(out=yc[:, ck(j)], in0=bank[4][:], scalar=-1.0 / D_CONV, in1=yc[:, ck(j)],
                                             op0=ALU.mult, op1=ALU.add).then_inc(cent_ready, 1)
                    if j >= 1:
                        add_square(Q_LN + j - 1, L)
                add_square(Q_LN + CC - 1, L)
                inverse(L, N_LN)
                dve.memset(sumsq[:], 0.0)
                split_lo(L, PC_ + 2, 0)
                wait_spread(L, N_LN)
                for j in range(CC + 1):
                    if j < CC:
                        dve.tensor_tensor(yc[:, ck(j)], yc[:, ck(j)], bank[5][:], ALU.mult).then_inc(norm_ready, 1)
                    if j >= 1:
                        dve.wait_ge(lnhi_ready, L * CC + j)
                        dve.tensor_tensor(cat_lo[:, ck(j - 1)], u[:, ck(j - 1)], cat_hi[:, ck(j - 1)].bitcast(F32),
                                          ALU.subtract).then_inc(lncat_ready, 1)

                for m in range(KC):
                    add_square(Q_MIX_POST + m, L)
                    if m in (1, 5):
                        split_lo(L, PC_ + 3 + m // 5, 0)

                def update_x(phase, n, split_x, splits):
                    inverse(L, n)
                    dve.memset(sumsq[:], 0.0)
                    wait_spread(L, n)
                    dve.wait_ge(m_ready, L * (2 * KC) + (phase + 1) * KC)
                    def scale_m(c):
                        dve.tensor_tensor(mT[:, ck(c)], mT[:, ck(c)], bank[POST_BANK][:], ALU.mult).then_inc(x_steps, 1)

                    scale_m(0)
                    for c in range(KC):
                        dve.wait_ge(x_steps, L * (4 * KC) + (2 * (phase * KC + c) + 1))
                        dve.tensor_tensor(x[:, ck(c)], x[:, ck(c)], mT[:, ck(c)], ALU.add).then_inc(x_steps, 1)
                        if c < KC - 1:
                            scale_m(c + 1)
                        if c >= 1:
                            split_x(c - 1)
                        if c in splits:
                            split_lo(L, splits[c], 0)
                    split_x(KC - 1)

                def h_lo_of_x(c):
                    dve.wait_ge(hhi_ready, L * (2 * KC) + (KC + c + 1))
                    dve.scalar_tensor_tensor(out=h_lo[:, ck(c)], in0=x[:, ck(c)], scalar=col(L, G_FFN_PRE + c),
                                             in1=h_hi[:, ck(c)].bitcast(F32), op0=ALU.mult, op1=ALU.subtract).then_inc(h_ready, 1)

                update_x(0, N_MIX_POST, h_lo_of_x, {SPLIT_UP_AT: PD + 1})
                for gap in (1, 2, 4):
                    for c in range(0, KC, 2 * gap):
                        if gap == 1:
                            dve.wait_ge(xsq_ready, L * KC + (c + 2))
                        last = dve.tensor_tensor(mT[:, ck(c)], mT[:, ck(c)], mT[:, ck(c + gap)], ALU.add)
                    if gap < 4:
                        dve.drain()
                last.then_inc(xsum_ready, 1)
                split_lo(L, PD + 2, 0)
                inverse(L, N_FFN_PRE)
                split_lo(L, PD + 3, 0)
                wait_spread(L, N_FFN_PRE)
                rstd = hx[0]
                dve.tensor_copy(rstd[:], bank[PRE_BANK][:])
                dve.drain()

                def mlp_chunk(i, s, banks, split=True):
                    ops = L * (4 * FC) + i * 8 + 4 * s
                    for n in range(2):
                        dve.wait_ge(unit_ready, L * NUNIT + i * 4 + (UD + 2 * s + n + 1) + START)
                        dve.tensor_tensor(z[n], bank[banks + n][:], rstd[:], ALU.mult).then_inc(z_ready, 1)
                    if split:
                        split_lo(L, PD + 2 + s, i)
                    for back in (1, 2):
                        for n in range(2):
                            dst, uc = (tap_gate, tap_value)[n], 2 * s + n
                            if back == 1:
                                dve.wait_ge(tap_ready, L * (2 * FC) + i * 4 + (uc + 1))
                                if n == 0:
                                    dve.wait_ge(z_ready, L * (2 * FC) + i * 4 + (2 * s + 2))
                            else:
                                dve.wait_ge(tap_ops, ops + (n + 1))
                            dve.scalar_tensor_tensor(
                                out=dst[:, back:T], in0=z[n][:, 0:T - back],
                                scalar=col(L, FW + uc * FTAPS + 2 - back, i * (4 * FTAPS)),
                                in1=dst[:, back:T], op0=ALU.mult, op1=ALU.add).then_inc(tap_ops, 1)
                    dve.wait_ge(tap_ops, ops + 4)
                    dve.wait_ge(gelu_ready, L * FC + i * 2 + (s + 1))
                    dve.tensor_tensor(hidden, gelu, tap_value, ALU.mult).then_inc(hidden_ready, 1)
                    dve.wait_ge(a_hi_ready, L * FC + i * 2 + (s + 1))
                    o = ds(i * (2 * T) + s * T, T)
                    dve.tensor_tensor(a_lo[:, o], hidden, a_hi[:, o].bitcast(F32), ALU.subtract).then_inc(a_ready, 1)

                mlp_chunk(0, 0, UP_BANKS[0], split=False)
                mlp_chunk(0, 1, 2, split=False)
                with dve.Fori(1, FC // 2) as i:
                    for s in range(2):
                        mlp_chunk(i, s, 2 * s)

                dve.wait_ge(p_hi_ready, L + 1)
                for k in range(PC):
                    c = KC - PC + k
                    dve.tensor_tensor(h_lo[:, ck(c)], praw[:, ck(k)], h_hi[:, ck(c)].bitcast(F32), ALU.subtract).then_inc(p_ready, 1)
                with dve.Fori(0, 2) as i:
                    for q in range(4):
                        split_lo(L, PE_ + 2 + 2 * q, i * 4, HALF_DOWN)
                        split_lo(L, PE_ + 3 + 2 * q, i * 4, HALF_DOWN)
                        add_square(Q_FFN_POST + q, L, i * 4)

                def x_lo(c):
                    dve.wait_ge(x_hi_ready, L * KC + (c + 1))
                    dve.tensor_tensor(h_lo[:, ck(c)], x[:, ck(c)], h_hi[:, ck(c)].bitcast(F32), ALU.subtract).then_inc(h_ready, 1)

                update_x(1, N_FFN_POST, x_lo, {SPLIT_GATE_AT[0]: PG, SPLIT_GATE_AT[1]: PG + 1})

                for m in range(KC):
                    if m in (2, 4, 6):
                        split_lo(L, PG + 1 + m // 2, 0)
                    if m >= 1:
                        add_square(Q_NEXT + m - 1, L)
                    dve.wait_ge(gate_ready, L * KC + (m + 1) + START)
                    dve.wait_ge(pw_ready, L * KC + KC)
                    dve.tensor_tensor(gate[m % 2][:], gate[m % 2][:], pw[:, ck(m)], ALU.mult)
                    dve.drain()
                    dve.tensor_tensor(x[:, ck(m)], x[:, ck(m)], gate[m % 2][:], ALU.add).then_inc(xg_new, 1)
                add_square(Q_NEXT + KC - 1, L)


def kernel(**inputs):
    import numpy as np
    import concourse.bacc as bacc
    from concourse.bass_utils import run_bass_kernel_spmd

    f32 = np.float32
    a = {k: np.asarray(v) for k, v in inputs.items()}

    def tiles(w, cols):
        c = w[:, cols:cols + P]
        return c.reshape(-1, P, P).transpose(1, 0, 2).reshape(P, -1)

    def unit_pairs(units):
        return [np.concatenate(units[n:n + 2], axis=1) for n in range(0, len(units), 2)]

    wa, wd, wp = [], [], []
    for L in range(DEPTH):
        w_in, w_out, up, down = a["w_in"][L], a["w_out"][L], a["ffn_up"][L], a["ffn_down"][L]
        units = []
        for j in range(CC):
            units += [tiles(w_in, j * P), tiles(w_in, D_CONV + j * P)]
        for h in range(NH):
            units += [tiles(w_in, 2 * D_CONV + g * NH * P + h * P) for g in range(4)]
        mix = [tiles(w_out, m * P) for m in range(KC)]
        conv_part, head_part = [t[:, :UNIT // 2] for t in mix], [t[:, UNIT // 2:] for t in mix]
        parts = head_part[:6] + conv_part[:6]
        units += [np.concatenate(parts[n:n + 2], axis=1) for n in range(0, 12, 2)] + mix[6:]
        for j in range(FC):
            units += [tiles(up, D_FF + j * P), tiles(up, j * P)]
        units += [tiles(a["ple_gate"][L], m * P) for m in range(KC)]
        wa += unit_pairs(units)
        wd.append(np.stack([tiles(down, m * P)[:, s * HALF_DOWN:(s + 1) * HALF_DOWN] for m in range(KC) for s in range(2)]))
        ple = [tiles(a["ple_proj"][L], m * P) for m in range(KC)]
        pad = np.zeros((P, HALF_DOWN - UNIT), f32)
        wp.append(np.stack([np.concatenate(ple[4 * s:4 * s + 4] + [pad], axis=1) for s in range(2)]))

    def cols(v):
        return np.ascontiguousarray(v.reshape(-1, P).T)

    params = []
    for L in range(DEPTH):
        cw = a["conv_w"][L].T.reshape(CC, P, TAPS).transpose(1, 0, 2).reshape(P, -1)
        fw = a["ffn_conv_w"][L].T.reshape(2, FC, P, FTAPS)[::-1].transpose(2, 1, 0, 3).reshape(P, -1)
        fb = a["ffn_conv_b"][L].reshape(2, FC, P)[::-1].transpose(2, 1, 0).reshape(P, -1)
        params += [cols(a[n][L]) for n in ("norm_mix_pre", "norm_mix_post", "norm_ffn_pre", "norm_ffn_post")]
        params += [cw, cols(a["conv_b"][L]), cols(a["conv_ln_g"][L]), cols(a["conv_ln_b"][L]), cols(a["ret_gn_g"][L]), fw, fb]
    params = np.concatenate(params, axis=1)

    n, m = np.arange(T)[None, :], np.arange(P)[:, None]
    masks = [np.where(n >= m, np.exp(np.log1p(-(2.0 ** (-5.0 - h))) * np.maximum(n - m, 0)), 0.0) * P ** -0.5 for h in range(NH)]
    inv_freq = f32(10000.0) ** (-(np.arange(P // 2, dtype=f32) / f32(P // 2)))
    consts = np.concatenate([np.eye(P) - 1.0 / P, np.eye(P), np.tile(inv_freq, 2)[:, None],
                                     np.repeat([-1.0, 1.0], P // 2)[:, None]], axis=1).astype(f32)

    arrays = {
        "xT": a["x"][0].T.reshape(KC, P, T),
        "pT": a["p"][:, 0].transpose(0, 2, 1).reshape(DEPTH, PC, P, T),
        "pos": a["positions"].reshape(1, T),
        "masks": np.concatenate(masks, axis=1).astype(f32), "consts": consts, "params": params,
        "wa": np.stack(wa + [np.zeros_like(wa[0])]), "wd": np.stack(wd), "wp": np.stack(wp),
    }
    arrays = {k: np.ascontiguousarray(v) for k, v in arrays.items()}
    nc = bacc.Bacc("TRN2", target_bir_lowering=False, num_devices=1, dynamic_dma_scratch_size=1024)
    aps = [nc.dram_tensor(k, v.shape, mybir.dt.from_np(v.dtype), kind="ExternalInput").ap() for k, v in arrays.items()]
    out = nc.dram_tensor("out", (KC, P, T), F32, kind="ExternalOutput").ap()
    build(nc, *aps, out)
    r = run_bass_kernel_spmd(nc, [arrays], core_ids=[0])
    y = r.results[0]["out"]
    return np.ascontiguousarray(y.reshape(DM, T).T)[None]
```
